# Optimizing a Trainium2 kernel written in Bass

```python
import math
import numpy as np
import jax
import jax.numpy as jnp
from jax import lax
import jax, jax.numpy as jnp

D_MODEL = 1024
BATCH = 1
SEQ = 256
DEPTH = 2

HEAD_DIM = 64
ROPE_THETA = 10000.0
NORM_EPS = 1e-6
D_FF = 4 * D_MODEL
Q_BLOCK = 128

A_HEADS = D_MODEL // (2 * HEAD_DIM)
IDX_HEADS = 4
DSA_TOPK = 256

B_HEADS = D_MODEL // (2 * HEAD_DIM)
B_KV_GROUPS = 2
CMP_BLOCK = 32
CMP_STRIDE = 16
CMP_HIDDEN = 256
SLC_BLOCK = 64
SLC_TOPN = 16
WINDOW = 512

C_HEADS = D_MODEL // (2 * HEAD_DIM)

EVEN_SPLITS = (A_HEADS * HEAD_DIM, HEAD_DIM, HEAD_DIM, IDX_HEADS * HEAD_DIM, HEAD_DIM, IDX_HEADS, B_HEADS * HEAD_DIM, 6 * B_KV_GROUPS * HEAD_DIM, 3 * B_HEADS)
EVEN_IN = sum(EVEN_SPLITS)
EVEN_MIX = (A_HEADS + B_HEADS) * HEAD_DIM
ODD_MIX = C_HEADS * 2 * HEAD_DIM
ODD_IN = 3 * ODD_MIX


def rms_norm(x, g):
    xf = x.astype(jnp.float32)
    y = xf * lax.rsqrt(jnp.mean(xf * xf, axis=-1, keepdims=True) + NORM_EPS)
    return (y * g.astype(jnp.float32)).astype(x.dtype)

def rope_tables(T):
    inv = 1.0 / (ROPE_THETA ** (jnp.arange(0, HEAD_DIM, 2, dtype=jnp.float32) / HEAD_DIM))
    ang = jnp.arange(T, dtype=jnp.float32)[:, None] * inv[None, :]
    return jnp.cos(ang), jnp.sin(ang)

def apply_rope(x, cos, sin):
    x1, x2 = jnp.split(x, 2, axis=-1)
    shape = (1, cos.shape[0]) + (1,) * (x.ndim - 3) + (cos.shape[1],)
    c = cos.reshape(shape).astype(x.dtype)
    s = sin.reshape(shape).astype(x.dtype)
    return jnp.concatenate([x1 * c - x2 * s, x2 * c + x1 * s], axis=-1)

def masked_softmax(s, mask):
    s = jnp.where(mask, s.astype(jnp.float32), -jnp.inf)
    m = jnp.max(s, axis=-1, keepdims=True)
    m = jnp.where(jnp.isfinite(m), m, 0.0)
    e = jnp.exp(s - m)
    return e / jnp.maximum(jnp.sum(e, axis=-1, keepdims=True), 1e-30)

def split_cols(a, sizes):
    offs = np.cumsum(sizes)[:-1].tolist()
    return jnp.split(a, offs, axis=-1)

def sweep_query_blocks(fn, T):
    nb = T // Q_BLOCK
    out = lax.map(fn, jnp.arange(nb))
    out = jnp.moveaxis(out, 0, 1)
    return out.reshape((out.shape[0], T) + out.shape[3:])

def dsa_attention(q, k, v, q_idx, k_idx, w_idx):
    T = q.shape[1]
    topk = min(DSA_TOPK, T // 4)
    scale = HEAD_DIM ** -0.5
    key_pos = jnp.arange(T)

    def block(i):
        t0 = i * Q_BLOCK
        tq = t0 + jnp.arange(Q_BLOCK)
        qb = lax.dynamic_slice_in_dim(q, t0, Q_BLOCK, 1)
        qib = lax.dynamic_slice_in_dim(q_idx, t0, Q_BLOCK, 1)
        wb = lax.dynamic_slice_in_dim(w_idx, t0, Q_BLOCK, 1)
        rel = jax.nn.relu(jnp.einsum('bqhd,bsd->bqhs', qib, k_idx).astype(jnp.float32))
        score = jnp.einsum('bqh,bqhs->bqs', wb.astype(jnp.float32), rel)
        score = jnp.where(key_pos[None, :] <= tq[:, None], score, -jnp.inf)
        _, idx = lax.top_k(score, topk)
        valid = idx <= tq[None, :, None]
        kg = jax.vmap(lambda kk, ii: kk[ii])(k, idx)
        vg = jax.vmap(lambda vv, ii: vv[ii])(v, idx)
        s = jnp.einsum('bqhd,bqkd->bhqk', qb, kg) * scale
        p = masked_softmax(s, valid[:, None])
        return jnp.einsum('bhqk,bqkd->bqhd', p.astype(vg.dtype), vg)

    return sweep_query_blocks(block, T)

def compress_blocks(x, pe, w1, w2):
    bsz, T, G, D = x.shape
    n_ch = T // CMP_STRIDE
    r = CMP_BLOCK // CMP_STRIDE
    n_c = n_ch - r + 1
    ch = x.reshape(bsz, n_ch, CMP_STRIDE, G, D)
    blk = jnp.concatenate([ch[:, j:j + n_c] for j in range(r)], axis=2)
    blk = blk + pe[None, None, :, None, :].astype(x.dtype)
    h = jax.nn.gelu(jnp.einsum('bnlgd,ldf->bngf', blk, w1.reshape(CMP_BLOCK, D, CMP_HIDDEN)))
    return jnp.einsum('bngf,fd->bngd', h, w2)

def slc_overlap(n_c, n_s):
    c0 = np.arange(n_c) * CMP_STRIDE
    c1 = c0 + CMP_BLOCK
    s0 = np.arange(n_s) * SLC_BLOCK
    s1 = s0 + SLC_BLOCK
    return ((c0[:, None] < s1[None, :]) & (c1[:, None] > s0[None, :])).astype(np.float32)

def nsa_attention(q, k_c, v_c, k_s, v_s, k_w, v_w, gate_logits, cmp_pe, cmp_w1, cmp_w2):
    bsz, T = q.shape[0], q.shape[1]
    G, J, D = B_KV_GROUPS, B_HEADS // B_KV_GROUPS, HEAD_DIM
    scale = D ** -0.5
    qg = q.reshape(bsz, T, G, J, D)
    g = jax.nn.sigmoid(gate_logits.astype(jnp.float32)).astype(q.dtype).reshape(bsz, T, G, J, 3)
    t_all = jnp.arange(T)

    kc = compress_blocks(k_c, cmp_pe[0], cmp_w1[0], cmp_w2[0])
    vc = compress_blocks(v_c, cmp_pe[1], cmp_w1[1], cmp_w2[1])
    n_c = kc.shape[1]
    cmp_end = jnp.arange(n_c) * CMP_STRIDE + CMP_BLOCK - 1
    s_c = jnp.einsum('btgjd,bngd->bgjtn', qg, kc) * scale
    p_c = masked_softmax(s_c, cmp_end[None, :] <= t_all[:, None])
    o_c = jnp.einsum('bgjtn,bngd->btgjd', p_c.astype(vc.dtype), vc)

    n_s = T // SLC_BLOCK
    n_sel = min(SLC_TOPN, n_s)
    imp = jnp.einsum('bgjtn,nm->bgtm', p_c, jnp.asarray(slc_overlap(n_c, n_s)))
    ks_blk = k_s.reshape(bsz, n_s, SLC_BLOCK, G, D).transpose(0, 3, 1, 2, 4)
    vs_blk = v_s.reshape(bsz, n_s, SLC_BLOCK, G, D).transpose(0, 3, 1, 2, 4)
    kw_pad = jnp.pad(k_w, ((0, 0), (WINDOW, 0), (0, 0), (0, 0)))
    vw_pad = jnp.pad(v_w, ((0, 0), (WINDOW, 0), (0, 0), (0, 0)))
    b_ix = jnp.arange(bsz)[:, None, None, None]
    g_ix = jnp.arange(G)[None, :, None, None]
    blk_ids = jnp.arange(n_s)

    def block(i):
        t0 = i * Q_BLOCK
        tq = t0 + jnp.arange(Q_BLOCK)
        qb = lax.dynamic_slice_in_dim(qg, t0, Q_BLOCK, 1)
        gq = lax.dynamic_slice_in_dim(g, t0, Q_BLOCK, 1)
        sc = lax.dynamic_slice_in_dim(imp, t0, Q_BLOCK, 2)
        cur = tq // SLC_BLOCK
        forced = (blk_ids[None, :] == 0) | (blk_ids[None, :] == cur[:, None]) | (blk_ids[None, :] == cur[:, None] - 1)
        admissible = blk_ids[None, :] * SLC_BLOCK <= tq[:, None]
        sc = jnp.where(forced, jnp.inf, sc)
        sc = jnp.where(admissible, sc, -jnp.inf)
        _, idx = lax.top_k(sc, n_sel)
        kg = ks_blk[b_ix, g_ix, idx]
        vg = vs_blk[b_ix, g_ix, idx]
        pos = idx[..., None] * SLC_BLOCK + jnp.arange(SLC_BLOCK)
        valid = (pos <= tq[None, None, :, None, None]).reshape(bsz, G, Q_BLOCK, n_sel * SLC_BLOCK)[:, :, None]
        s_s = jnp.einsum('bqgjd,bgqnsd->bgjqns', qb, kg).reshape(bsz, G, J, Q_BLOCK, n_sel * SLC_BLOCK) * scale
        p_s = masked_softmax(s_s, valid)
        o_s = jnp.einsum('bgjqk,bgqkd->bqgjd', p_s.astype(vg.dtype), vg.reshape(bsz, G, Q_BLOCK, n_sel * SLC_BLOCK, D))
        kw = lax.dynamic_slice_in_dim(kw_pad, t0, WINDOW + Q_BLOCK, 1)
        vw = lax.dynamic_slice_in_dim(vw_pad, t0, WINDOW + Q_BLOCK, 1)
        pos_w = t0 - WINDOW + jnp.arange(WINDOW + Q_BLOCK)
        valid_w = (pos_w[None, :] >= 0) & (pos_w[None, :] <= tq[:, None]) & (pos_w[None, :] > tq[:, None] - WINDOW)
        s_w = jnp.einsum('bqgjd,bsgd->bgjqs', qb, kw) * scale
        p_w = masked_softmax(s_w, valid_w)
        o_w = jnp.einsum('bgjqs,bsgd->bqgjd', p_w.astype(vw.dtype), vw)
        return gq[..., 1:2] * o_s + gq[..., 2:3] * o_w

    o_sw = sweep_query_blocks(block, T)
    o = g[..., 0:1] * o_c + o_sw
    return o.reshape(bsz, T, B_HEADS, D)

def even_mixer(h, w_in, cmp_pe, cmp_w1, cmp_w2, w_out, cos, sin):
    bsz, T, _ = h.shape
    proj = jnp.einsum('btd,de->bte', h, w_in)
    qa, ka, va, qi, ki, wi, qb, kvb, gb = split_cols(proj, EVEN_SPLITS)
    qa = apply_rope(qa.reshape(bsz, T, A_HEADS, HEAD_DIM), cos, sin)
    ka = apply_rope(ka, cos, sin)
    qi = apply_rope(qi.reshape(bsz, T, IDX_HEADS, HEAD_DIM), cos, sin)
    ki = apply_rope(ki, cos, sin)
    o_a = dsa_attention(qa, ka, va, qi, ki, wi)
    qb = apply_rope(qb.reshape(bsz, T, B_HEADS, HEAD_DIM), cos, sin)
    kvb = kvb.reshape(bsz, T, 6, B_KV_GROUPS, HEAD_DIM)
    k_c = apply_rope(kvb[:, :, 0], cos, sin)
    v_c = kvb[:, :, 1]
    k_s = apply_rope(kvb[:, :, 2], cos, sin)
    v_s = kvb[:, :, 3]
    k_w = apply_rope(kvb[:, :, 4], cos, sin)
    v_w = kvb[:, :, 5]
    o_b = nsa_attention(qb, k_c, v_c, k_s, v_s, k_w, v_w, gb, cmp_pe, cmp_w1, cmp_w2)
    o = jnp.concatenate([o_a.reshape(bsz, T, -1), o_b.reshape(bsz, T, -1)], axis=-1)
    return jnp.einsum('bte,ed->btd', o, w_out)

def diff_mixer(h, w_in, lam, subln_g, w_out, cos, sin, lambda_init):
    bsz, T, _ = h.shape
    proj = jnp.einsum('btd,de->bte', h, w_in)
    q, k, v = jnp.split(proj, 3, axis=-1)
    q = apply_rope(q.reshape(bsz, T, C_HEADS * 2, HEAD_DIM), cos, sin).reshape(bsz, T, C_HEADS, 2, HEAD_DIM)
    k = apply_rope(k.reshape(bsz, T, C_HEADS * 2, HEAD_DIM), cos, sin).reshape(bsz, T, C_HEADS, 2, HEAD_DIM)
    v = v.reshape(bsz, T, C_HEADS, 2 * HEAD_DIM)
    lf = lam.astype(jnp.float32)
    lam_val = jnp.exp(jnp.sum(lf[0] * lf[1])) - jnp.exp(jnp.sum(lf[2] * lf[3])) + lambda_init
    scale = HEAD_DIM ** -0.5
    key_pos = jnp.arange(T)

    def block(i):
        t0 = i * Q_BLOCK
        tq = t0 + jnp.arange(Q_BLOCK)
        qb = lax.dynamic_slice_in_dim(q, t0, Q_BLOCK, 1)
        s = jnp.einsum('bqhcd,bshcd->bhcqs', qb, k) * scale
        p = masked_softmax(s, key_pos[None, :] <= tq[:, None])
        a = p[:, :, 0] - lam_val * p[:, :, 1]
        return jnp.einsum('bhqs,bshe->bqhe', a.astype(v.dtype), v)

    o = sweep_query_blocks(block, T)
    o = rms_norm(o, subln_g) * (1.0 - lambda_init)
    return jnp.einsum('bte,ed->btd', o.reshape(bsz, T, ODD_MIX), w_out)

def sq_relu_mlp(h, w_up, w_down):
    u = jnp.einsum('btd,df->btf', h, w_up)
    return jnp.einsum('btf,fd->btd', jnp.square(jax.nn.relu(u)), w_down)

def first_inputs(seed: int = 0) -> dict:
    key = jax.random.key(seed)
    ks = jax.random.split(key, 16)
    ne = (DEPTH + 1) // 2
    no = DEPTH // 2

    def nrm(k, shape, fan_in):
        return jax.random.normal(k, shape, jnp.float32) * (fan_in ** -0.5)

    def gain(k, shape):
        return 1.0 + 0.05 * jax.random.normal(k, shape, jnp.float32)

    return {
        'x': jax.random.normal(ks[0], (BATCH, SEQ, D_MODEL), jnp.float32),
        'mix_norm_g': gain(ks[1], (DEPTH, D_MODEL)),
        'mlp_norm_g': gain(ks[2], (DEPTH, D_MODEL)),
        'even_w_in': nrm(ks[3], (ne, D_MODEL, EVEN_IN), D_MODEL),
        'even_cmp_pe': 0.02 * jax.random.normal(ks[4], (ne, 2, CMP_BLOCK, HEAD_DIM), jnp.float32),
        'even_cmp_w1': nrm(ks[5], (ne, 2, CMP_BLOCK * HEAD_DIM, CMP_HIDDEN), CMP_BLOCK * HEAD_DIM),
        'even_cmp_w2': nrm(ks[6], (ne, 2, CMP_HIDDEN, HEAD_DIM), CMP_HIDDEN),
        'even_w_out': nrm(ks[7], (ne, EVEN_MIX, D_MODEL), EVEN_MIX),
        'odd_w_in': nrm(ks[8], (no, D_MODEL, ODD_IN), D_MODEL),
        'odd_lambda': 0.1 * jax.random.normal(ks[9], (no, 4, HEAD_DIM), jnp.float32),
        'odd_subln_g': gain(ks[10], (no, 2 * HEAD_DIM)),
        'odd_w_out': nrm(ks[11], (no, ODD_MIX, D_MODEL), ODD_MIX),
        'mlp_w_up': nrm(ks[12], (DEPTH, D_MODEL, D_FF), D_MODEL),
        'mlp_w_down': nrm(ks[13], (DEPTH, D_FF, D_MODEL), D_FF),
        'final_norm_g': gain(ks[14], (D_MODEL,)),
    }

def first_block(x, mix_norm_g, mlp_norm_g, even_w_in, even_cmp_pe, even_cmp_w1, even_cmp_w2, even_w_out, odd_w_in, odd_lambda, odd_subln_g, odd_w_out, mlp_w_up, mlp_w_down, final_norm_g):
    T = x.shape[1]
    cos, sin = rope_tables(T)
    h = x
    for layer in range(DEPTH):
        u = rms_norm(h, mix_norm_g[layer])
        if layer % 2 == 0:
            e = layer // 2
            h = h + even_mixer(u, even_w_in[e], even_cmp_pe[e], even_cmp_w1[e], even_cmp_w2[e], even_w_out[e], cos, sin)
        else:
            o = layer // 2
            lambda_init = 0.8 - 0.6 * math.exp(-0.3 * layer)
            h = h + diff_mixer(u, odd_w_in[o], odd_lambda[o], odd_subln_g[o], odd_w_out[o], cos, sin, lambda_init)
        h = h + sq_relu_mlp(rms_norm(h, mlp_norm_g[layer]), mlp_w_up[layer], mlp_w_down[layer])
    return rms_norm(h, final_norm_g)


N_MIXERS = 2
N_POOL_LAYERS = (DEPTH + 1) // 2
N_MOBA_LAYERS = DEPTH // 2
POOL_WINDOWS = (2, 4, 8, 16)
N_POOL_GROUPS = len(POOL_WINDOWS)
POOL_GROUP = D_MODEL // N_POOL_GROUPS
N_HEADS = D_MODEL // HEAD_DIM
MOBA_BLOCK = 256
MOBA_TOPK = 3
Q_CHUNK = 128
NUM_BUCKETS = 32
MAX_DISTANCE = 1024
D_FF_2 = 4 * D_MODEL
EPS = 1e-6


def rmsnorm(x, g):
    xf = x.astype(jnp.float32)
    y = xf * lax.rsqrt(jnp.mean(xf * xf, axis=-1, keepdims=True) + EPS)
    return (y * g.astype(jnp.float32)).astype(x.dtype)

def modulate(h, shift, scale):
    return h * (1 + scale[:, None, :]) + shift[:, None, :]

def t5_bucket(dist):
    max_exact = NUM_BUCKETS // 2
    nf = jnp.maximum(dist, 1).astype(jnp.float32)
    large = max_exact + (jnp.log(nf / max_exact) / math.log(MAX_DISTANCE / max_exact)
                         * (NUM_BUCKETS - max_exact)).astype(jnp.int32)
    large = jnp.minimum(large, NUM_BUCKETS - 1)
    return jnp.where(dist < max_exact, dist, large)

def pool_mixer(h, w_pool, pool_scale):
    B, S, D = h.shape
    hf = h.astype(jnp.float32)
    cs = jnp.concatenate([jnp.zeros((B, 1, D), jnp.float32), jnp.cumsum(hf, axis=1)], axis=1)
    t = jnp.arange(S)
    groups = []
    for g, w in enumerate(POOL_WINDOWS):
        sl = slice(g * POOL_GROUP, (g + 1) * POOL_GROUP)
        cs_g = cs[:, :, sl]
        lo = jnp.maximum(t + 1 - w, 0)
        win_sum = cs_g[:, 1:] - jnp.take(cs_g, lo, axis=1)
        cnt = jnp.minimum(t + 1, w).astype(jnp.float32)[None, :, None]
        groups.append(win_sum / cnt - hf[:, :, sl])
    pooled = jnp.stack(groups, axis=2)
    y = jnp.einsum('bsgi,gio->bsgo', pooled, w_pool.astype(jnp.float32)).reshape(B, S, D)
    return (y * pool_scale.astype(jnp.float32)).astype(h.dtype)

def moba_attention(h, w_qkv, w_o, rel_bias):
    B, S, D = h.shape
    H, Dh, BL = N_HEADS, HEAD_DIM, MOBA_BLOCK
    qkv = h @ w_qkv
    q, k, v = jnp.split(qkv, 3, axis=-1)
    q = q.reshape(B, S, H, Dh).transpose(0, 2, 1, 3)
    k = k.reshape(B, S, H, Dh).transpose(0, 2, 1, 3)
    v = v.reshape(B, S, H, Dh).transpose(0, 2, 1, 3)
    nb = -(-S // BL)
    pad = nb * BL - S
    kb = jnp.pad(k, ((0, 0), (0, 0), (0, pad), (0, 0))).reshape(B, H, nb, BL, Dh)
    vb = jnp.pad(v, ((0, 0), (0, 0), (0, pad), (0, 0))).reshape(B, H, nb, BL, Dh)
    kmean = jnp.mean(kb.astype(jnp.float32), axis=3)
    top = min(MOBA_TOPK, nb - 1)
    scale = HEAD_DIM ** -0.5
    rb = rel_bias.astype(jnp.float32)
    rbT = rb.T
    bi = jnp.arange(B)[:, None, None]
    hi = jnp.arange(H)[None, :, None]
    hi4 = jnp.arange(H)[None, :, None, None]
    n_chunks = S // Q_CHUNK

    def chunk_fn(ci):
        s0 = ci * Q_CHUNK
        qf = lax.dynamic_slice_in_dim(q, s0, Q_CHUNK, axis=2).astype(jnp.float32)
        tq = s0 + jnp.arange(Q_CHUNK)
        own = s0 // BL
        k_own = lax.dynamic_index_in_dim(kb, own, axis=2, keepdims=False)
        v_own = lax.dynamic_index_in_dim(vb, own, axis=2, keepdims=False)
        dist_own = tq[:, None] - (own * BL + jnp.arange(BL))[None, :]
        bias_own = rb[t5_bucket(jnp.maximum(dist_own, 0))].transpose(2, 0, 1)[None]
        logit_own = jnp.einsum('bhqd,bhkd->bhqk', qf, k_own.astype(jnp.float32)) * scale + bias_own
        logit_own = jnp.where((dist_own >= 0)[None, None], logit_own, -jnp.inf)
        logits = []
        sel = []
        if top > 0:
            gate = jnp.einsum('bhqd,bhnd->bhqn', qf, kmean)
            past = jnp.arange(nb) < own
            gate = jnp.where(past[None, None, None], gate, -jnp.inf)
            _, idx = lax.top_k(gate, top)
            for r in range(top):
                idx_r = idx[..., r]
                k_sel = kb[bi, hi, idx_r]
                kpos = idx_r[..., None] * BL + jnp.arange(BL)
                dist = tq[None, None, :, None] - kpos
                bias_r = rbT[hi4, t5_bucket(jnp.maximum(dist, 0))]
                lg = jnp.einsum('bhqd,bhqkd->bhqk', qf, k_sel.astype(jnp.float32)) * scale + bias_r
                lg = jnp.where((idx_r < own)[..., None], lg, -jnp.inf)
                logits.append(lg)
                sel.append(idx_r)
        logits.append(logit_own)
        p = jax.nn.softmax(jnp.concatenate(logits, axis=-1), axis=-1)
        out = jnp.einsum('bhqk,bhkd->bhqd', p[..., top * BL:], v_own.astype(jnp.float32))
        for r in range(top):
            v_sel = vb[bi, hi, sel[r]]
            out = out + jnp.einsum('bhqk,bhqkd->bhqd', p[..., r * BL:(r + 1) * BL],
                                   v_sel.astype(jnp.float32))
        return out.astype(h.dtype)

    o = lax.map(chunk_fn, jnp.arange(n_chunks))
    o = o.transpose(1, 0, 3, 2, 4).reshape(B, S, D)
    return o @ w_o

def squared_relu_mlp(h, w_up, w_down):
    a = jax.nn.relu(h @ w_up)
    return (a * a) @ w_down

def second_inputs(seed: int = 0) -> dict:
    key = jax.random.key(seed)
    ks = jax.random.split(key, 16)
    f32 = jnp.float32
    D = D_MODEL
    nrm = lambda k, shape, s: jax.random.normal(k, shape, f32) * s
    return {
        "x": nrm(ks[0], (BATCH, SEQ, D), 1.0),
        "c": nrm(ks[1], (BATCH, D), 1.0),
        "rel_bias": nrm(ks[2], (NUM_BUCKETS, N_HEADS), 0.5),
        "w_mod": nrm(ks[3], (DEPTH, D, 6 * D), 0.5 * D ** -0.5),
        "b_mod": nrm(ks[4], (DEPTH, 6 * D), 0.02),
        "norm_mix": 1.0 + nrm(ks[5], (DEPTH, D), 0.02),
        "norm_mlp": 1.0 + nrm(ks[6], (DEPTH, D), 0.02),
        "w_pool": nrm(ks[7], (N_POOL_LAYERS, N_POOL_GROUPS, POOL_GROUP, POOL_GROUP), POOL_GROUP ** -0.5),
        "pool_scale": 1.0 + nrm(ks[8], (N_POOL_LAYERS, D), 0.05),
        "w_qkv": nrm(ks[9], (N_MOBA_LAYERS, D, 3 * D), D ** -0.5),
        "w_o": nrm(ks[10], (N_MOBA_LAYERS, D, D), D ** -0.5),
        "w_up": nrm(ks[11], (DEPTH, D, D_FF_2), D ** -0.5),
        "w_down": nrm(ks[12], (DEPTH, D_FF_2, D), D_FF_2 ** -0.5),
        "norm_final": 1.0 + nrm(ks[13], (D,), 0.02),
    }

def second_block(x, c, rel_bias, w_mod, b_mod, norm_mix, norm_mlp, w_pool, pool_scale,
              w_qkv, w_o, w_up, w_down, norm_final):
    c_act = jax.nn.silu(c)
    for i in range(DEPTH):
        mod = c_act @ w_mod[i] + b_mod[i]
        sh1, sc1, g1, sh2, sc2, g2 = jnp.split(mod, 6, axis=-1)
        h = modulate(rmsnorm(x, norm_mix[i]), sh1, sc1)
        if i % N_MIXERS == 0:
            y = pool_mixer(h, w_pool[i // N_MIXERS], pool_scale[i // N_MIXERS])
        else:
            y = moba_attention(h, w_qkv[i // N_MIXERS], w_o[i // N_MIXERS], rel_bias)
        x = x + g1[:, None, :] * y
        h = modulate(rmsnorm(x, norm_mlp[i]), sh2, sc2)
        x = x + g2[:, None, :] * squared_relu_mlp(h, w_up[i], w_down[i])
    return rmsnorm(x, norm_final)


def setup_inputs(seed=0):
    out = dict(first_inputs(seed))
    for name, value in second_inputs(seed + 1).items():
        if name != "x":
            out[name + "_2"] = value
    return out


def reference(
    x, mix_norm_g, mlp_norm_g, even_w_in, even_cmp_pe, even_cmp_w1, even_cmp_w2, even_w_out,
    odd_w_in, odd_lambda, odd_subln_g, odd_w_out, mlp_w_up, mlp_w_down, final_norm_g, c_2,
    rel_bias_2, w_mod_2, b_mod_2, norm_mix_2, norm_mlp_2, w_pool_2, pool_scale_2, w_qkv_2,
    w_o_2, w_up_2, w_down_2, norm_final_2,
):
    x = first_block(
        x, mix_norm_g, mlp_norm_g, even_w_in, even_cmp_pe, even_cmp_w1, even_cmp_w2, even_w_out,
        odd_w_in, odd_lambda, odd_subln_g, odd_w_out, mlp_w_up, mlp_w_down, final_norm_g,
    )
    return second_block(
        x, c_2, rel_bias_2, w_mod_2, b_mod_2, norm_mix_2, norm_mlp_2, w_pool_2, pool_scale_2,
        w_qkv_2, w_o_2, w_up_2, w_down_2, norm_final_2,
    )


_drawn_inputs = setup_inputs


def setup_inputs(seed=0):
    import zlib

    import numpy as np

    out = dict(_drawn_inputs(seed))
    spreads = {}
    factors = {'even_cmp_pe': 8.0,
     'odd_lambda': 8.0,
     'norm_mix_2': 8.0,
     'norm_mlp_2': 4.654,
     'pool_scale_2': 4.25,
     'norm_final_2': 7.892,
     'rel_bias_2': 4.937}
    for name, (base, spread) in spreads.items():
        noise = np.random.default_rng([zlib.crc32(name.encode()), seed]).standard_normal(out[name].shape)
        drawn = base * np.exp(spread * noise) if base else spread * noise
        out[name] = jnp.asarray(drawn.astype(out[name].dtype))
    for name, factor in factors.items():
        out[name] = (out[name] * factor).astype(out[name].dtype)
    return out
```

```python
import concourse.bass as bass
from concourse import mybir
from contextlib import ExitStack
import math
import numpy as np

T = 256
D = 1024
KB = D // 128
NT = T // 128
HD = 64
FF = 4 * D
EPS = 1e-6
SPLIT = 2048
RING = 4
NEG = -1e30
MARK = -3e38
TOPK = min(256, T // 4)
NBLK = 15
CW = 8 * NBLK
LAM_INIT = 0.8 - 0.6 * math.exp(-0.3)

C_ID, C_SW, C_FLIP, C_TRI = 0, 128, 256, 384
C_COS, C_SIN, C_COSQ, C_SINQ = 512, 768, 1024, 1280
C_CORR = 1536
C_HB = C_CORR + 128
C_CMP = C_HB + 8
C_END = C_CMP + NT * NBLK

QA, QI, KA, KI, QB, KC, VC, KS, KW = 0, 4, 6, 7, 8, 12, 13, 14, 15

V_MIX, V_MLP, V_FIN, V_MIX2, V_MLP2, V_FIN2, V_POOL, V_C, V_SUB = 0, 16, 32, 40, 56, 72, 80, 88, 96
NV = 97

EVEN, MLP0, DIFF, MLP1, POOL, MLP2, MOBA, MLP3, LAST = 0, 14, 46, 62, 94, 95, 127, 143, 175
MLPS = (MLP0, MLP1, MLP2, MLP3)
NPLAIN = 4
PLAIN_AT = 10
EVENT_OF_MLP = (2, 4, 7, 9)


def raw_index(m):
    return m if m < PLAIN_AT else m + NPLAIN


def up_idx(s):
    return max(0, 2 * s - 1)


def dn_idx(s):
    return min(2 * s + 2, 31)


def build(nc, a):
    fp32, f32r, bf16 = mybir.dt.float32, mybir.dt.float32r, mybir.dt.bfloat16
    ALU, ACT, AX = mybir.AluOpType, mybir.ActivationFunctionType, mybir.AxisListType
    ctx = ExitStack()
    with ctx:
        def sb(name, shape, dt=fp32):
            return ctx.enter_context(nc.sbuf_tensor(name, shape, dt))

        def sem(name):
            return ctx.enter_context(nc.semaphore(name))

        raw = sb("raw", [128, RING, SPLIT])
        whi = sb("whi", [128, RING, SPLIT], f32r)
        wlo = sb("wlo", [128, RING, SPLIT], f32r)
        xT = sb("xT", [128, KB, T])
        u = sb("u", [128, KB, T])
        uh = sb("uh", [128, KB, T], f32r)
        ul = sb("ul", [128, KB, T], f32r)
        work = sb("work", [128, 4, 512])
        hh = sb("hh", [128, 2, 512], f32r)
        hl = sb("hl", [128, 2, 512], f32r)
        qk = sb("qk", [128, 16, T])
        vo = sb("vo", [128, 2, NT, D])
        P = sb("P", [128, 4, 384])
        PT = sb("PT", [128, 2, 384])
        con = sb("con", [128, C_END])
        ones = sb("ones", [128, 128])
        zero8 = sb("zero8", [128, KB])
        idb = sb("idb", [128, 128], bf16)
        trib = sb("trib", [128, 128], bf16)
        vec = sb("vec", [128, NV])
        bpe = sb("bpe", [128, 128])
        mod = sb("mod", [128, 96])
        gain = sb("gain", [128, 4, KB])
        gpool = sb("gpool", [128, KB])
        cact = sb("cact", [128, KB])
        rstd = sb("rstd", [128, T])
        var = sb("var", [128, T])
        tk = sb("tk", [128, NT, 92])
        score = sb("score", [128, 384])
        sel = sb("sel", [128, 384], bf16)
        top8 = sb("top8", [128, NT, 8])
        nmax = sb("nmax", [128, 24, 2])
        sums = sb("sums", [128, 24, 2])
        rs = sb("rs", [128, 24, 2])
        gates = sb("gates", [128, NT, 24])
        lam = sb("lam", [128, 8])
        w2 = sb("w2", [128, 2, 192])
        hT = sb("hT", [128, 4, 30])
        kcm = sb("kcm", [128, 30])
        cst = sb("cst", [128, 6, NT * 8])
        msq = sb("msq", [128, NT, 8])
        bank = [ctx.enter_context(nc.psum_tensor(f"bank{i}", [128, 512], fp32)) for i in range(8)]
        gdram = nc.dram_tensor("bias_rows", [16, 384], fp32, kind="Internal").ap()

        ident = con[:, C_ID:C_ID + 128]
        swap = con[:, C_SW:C_SW + 128]
        flip = con[:, C_FLIP:C_FLIP + 128]
        tri = con[:, C_TRI:C_TRI + 128]
        one_col = ones[:, 0:1]
        v_ = vo[:, 0, :, :]
        o_ = vo[:, 1, :, :]
        acc = [vo[:, j, :, :].rearrange("p t n -> p (t n)") for j in range(2)]
        stage = [qk[:, 8 * j:8 * j + 8, :].rearrange("p b n -> p (b n)") for j in range(2)]
        uf = u[:, :, :].rearrange("p b n -> p (b n)")
        kc2 = uf[:, 0:1024].rearrange("p (c t) -> p c t", c=4)
        blk = uf[:, 1024:1984].rearrange("p (c l n) -> p c l n", c=2, l=16)
        hank = u
        hact, htmp = work[0:30, 0, :], work[0:30, 1, :]
        rows = work[:, 0, 0:128]
        rows2 = work[:, 0, 128:256]
        relb = work[0:32, 1, 0:16]
        hot = work[0:32, 1, 128:512]
        gmask = work[0:16, 2, 0:384]
        out2 = vo[:, 0, :, :]
        gb = PT[0:16, 0, :]
        lamw = P[:, 0, 0:256].rearrange("p (a n) -> p a n", a=4)
        lamp = P[:, 1, 0:128].rearrange("p (a n) -> p a n", a=2)
        vbd = v_[:, 0, 256:768].rearrange("p (h n) -> p h n", h=8)
        gtmp = v_[:, 0, 768:1008].rearrange("p (a n) -> p a n", a=2)
        pcT = v_[:, 1, 256:512].rearrange("p (t n) -> p t n", t=NT)
        pc = v_[:, 1, 512:752].rearrange("p (t n) -> p t n", t=NT)
        hrep = v_[:, 1, 752:992].rearrange("p (a n) -> p a n", a=2)

        loaded = [sem(f"loaded{i}") for i in range(RING)]
        hi_ready, lo_ready, used, plain_used = sem("hi_ready"), sem("lo_ready"), sem("used"), sem("plain_used")
        in_x, in_con, in_rows, in_misc, in_w2 = sem("in_x"), sem("in_con"), sem("in_rows"), sem("in_misc"), sem("in_w2")
        zeroed, vec_T, vec_ready, x_T = sem("zeroed"), sem("vec_T"), sem("vec_ready"), sem("x_T")
        acc_ready, x_ready, sq_ready, sumsq_ready = sem("acc_ready"), sem("x_ready"), sem("sq_ready"), sem("sumsq_ready")
        rv_ready, rstd_ready = sem("rv_ready"), sem("rstd_ready")
        u_ready, uh_ready, ul_ready = sem("u_ready"), sem("uh_ready"), sem("ul_ready")
        dchain, achain = sem("dchain"), sem("achain")
        relu_done, h_done, hh_done, hl_done = sem("relu_done"), sem("h_done"), sem("hh_done"), sem("hl_done")
        st_loaded = [sem(f"st_loaded{j}") for j in range(2)]
        st_done = [sem(f"st_done{j}") for j in range(2)]
        mod_T, mod_ready = sem("mod_T"), sem("mod_ready")
        bias_T, bias_sb, bias_out = sem("bias_T"), sem("bias_sb"), sem("bias_out")
        oT_ready, oh_ready, ol_ready, o_ready = sem("oT_ready"), sem("oh_ready"), sem("ol_ready"), sem("o_ready")
        e_free, e_t2, e_sw, e_add = sem("e_free"), sem("e_t2"), sem("e_sw"), sem("e_add")
        e_is, e_ir, e_ia, e_sel = sem("e_is"), sem("e_ir"), sem("e_ia"), sem("e_sel")
        kc2_in, blk_ready, hT_ps, g_sq, g_in, g_th, h_act, hT_ready = (
            sem("kc2_in"), sem("blk_ready"), sem("hT_ps"), sem("g_sq"), sem("g_in"), sem("g_th"), sem("h_act"),
            sem("hT_ready"))
        kv_ps, kv_ready, sc_ps, sc_sub, sc_exp, pc_ready, pc_ps, pcT_ready, oc_ps = (
            sem("kv_ps"), sem("kv_ready"), sem("sc_ps"), sem("sc_sub"), sem("sc_exp"), sem("pc_ready"),
            sem("pc_ps"), sem("pcT_ready"), sem("oc_ps"))
        gate_in, gate_exp = sem("gate_in"), sem("gate_exp")
        o_free = sem("o_free")
        d_t2, d_sw, d_add, d_v = sem("d_t2"), sem("d_sw"), sem("d_add"), sem("d_v")
        d_sq, d_rv, d_rt = sem("d_sq"), sem("d_rv"), sem("d_rt")
        b_copied = sem("b_copied")
        h_in = [sem(f"h_in{i}") for i in range(8)]
        p_h, p_sum, p_hi = sem("p_h"), sem("p_sum"), sem("p_hi")
        s_ps = {ph: sem(f"s_ps_{ph}") for ph in "edb"}
        s_max = {ph: sem(f"s_max_{ph}") for ph in "edb"}
        s_exp = {ph: sem(f"s_exp_{ph}") for ph in "edb"}
        s_tr = {ph: sem(f"s_tr_{ph}") for ph in "edb"}
        s_pt = {ph: sem(f"s_pt_{ph}") for ph in "edb"}
        s_pv = {ph: sem(f"s_pv_{ph}") for ph in "edb"}
        s_cmb = sem("s_cmb")
        lam_in, lam_exp = sem("lam_in"), sem("lam_exp")
        fin_T, fin_act, fin_dve, out_done = sem("fin_T"), sem("fin_act"), sem("fin_dve"), sem("out_done")

        def acc_no(e):
            return 4 * (e if e < 5 else e - 1)

        def u_no(e):
            return 8 * (e if e < 4 else e - 1)

        def ul_no(e):
            return 8 * (e if e < 4 else e - 2)

        def up_src(l, s):
            return a["up"][l][:, bass.ds(s * 256, 256)].rearrange("(k p) n -> p k n", p=128)

        def dn_src(l, s):
            return a["down"][l][bass.ds(s * 256, 256), :].rearrange("(k p) n -> p k n", p=128)

        def even_map(i):
            kind, h = i // 8, i % 8
            if kind == 0:
                return QA + h // 2, 64 * (h % 2), KA, tk, slice(0, 64), (4, 5)
            g, j = h // 4, h % 4
            vs = 128 * (kind - 1) + 64 * g
            return QB + j, 64 * g, (KS, KW)[kind - 1], v_, slice(vs, vs + 64), ((6, 7), (4, 5))[kind - 1]

        block = ctx.enter_context(nc.Block())

        @block.sync
        def _(sp):
            sp.dma_start(o_[:, :, :], a["x"].rearrange("(t p) n -> p t n", p=128)).then_inc(in_x, 16)
            sp.dma_start(con[:, :], a["con"]).then_inc(in_con, 16)

            def slot_of(m):
                n = raw_index(m)
                if PLAIN_AT <= n - RING < PLAIN_AT + NPLAIN:
                    sp.wait_ge(plain_used, n - RING - PLAIN_AT + 1)
                elif n >= RING:
                    sp.wait_ge(lo_ready, n - RING + 1 if n < PLAIN_AT else m - RING + 1)
                return raw[:, n % RING, :], loaded[n % RING]

            def load(m, src, k=KB):
                dst, s = slot_of(m)
                sp.dma_start(dst.rearrange("p (k n) -> p k n", k=k), src).then_inc(s, 16)

            def cols(w, c0, n=256):
                return w[:, c0:c0 + n].rearrange("(k p) n -> p k n", p=128)

            w = a["even_in"]
            load(0, cols(w, 640))
            sp.wait_ge(in_rows, 16 * 11)
            dst, s = slot_of(1)
            d4 = dst.rearrange("p (k n) -> p k n", k=KB)
            for i, c0 in enumerate((512, 512, 896, 896)):
                sp.dma_start(d4[:, :, 64 * i:64 * i + 64], cols(w, c0, 64)).then_inc(s, 16)
            dst, s = slot_of(2)
            d4 = dst[:, 0:KB * 92].rearrange("p (k n) -> p k n", k=KB)
            for d0, c0, n in ((0, 576, 64), (64, 960, 4), (68, 2244, 24)):
                sp.dma_start(d4[:, :, d0:d0 + n], cols(w, c0, n)).then_inc(s, 16)
            load(3, cols(w, 0))
            load(4, cols(w, 256))
            load(5, cols(w, 1476))
            for i in range(2):
                dst, s = slot_of(6 + i)
                d4 = dst.rearrange("p (k n) -> p k n", k=KB)
                for j in range(2):
                    for g in range(2):
                        c = 128 * j + 64 * g
                        sp.dma_start(d4[:, :, c:c + 64], cols(w, 964 + 256 * g + 64 * (2 * i + j), 64)).then_inc(s, 16)
            load(8, cols(w, 1732))
            load(9, cols(w, 1988))
            for i in range(NPLAIN):
                n = PLAIN_AT + i
                sp.wait_ge(lo_ready, n - RING + 1)
                sp.dma_start(raw[:, n % RING, :].rearrange("p (k n) -> p k n", k=KB),
                             cols(a["cmp_w1"][i // 2][1024 * (i % 2):1024 * (i % 2) + 1024, :], 0))\
                    .then_inc(loaded[n % RING], 16)
            for c in range(4):
                load(10 + c, cols(a["even_out"], 256 * c))

            def mlp(l):
                m0 = MLPS[l]
                load(m0, up_src(l, 0))
                for i in range(1, 5):
                    if i % 2:
                        load(m0 + i, up_src(l, (i + 1) // 2))
                    else:
                        load(m0 + i, dn_src(l, i // 2 - 1), 2)
                with sp.Fori(1, 7) as it:
                    for i in range(1, 5):
                        m = m0 + i
                        n = raw_index(m)
                        sp.wait_ge(lo_ready, it * 4 + (m - RING + 1))
                        up = i % 2 == 1
                        sp.dma_start(raw[:, n % RING, :].rearrange("p (k n) -> p k n", k=KB if up else 2),
                                     up_src(l, it * 2 + (i + 1) // 2) if up else dn_src(l, it * 2 + (i // 2 - 1)))\
                            .then_inc(loaded[n % RING], 16)
                load(m0 + 29, up_src(l, 15))
                load(m0 + 30, dn_src(l, 14), 2)
                load(m0 + 31, dn_src(l, 15), 2)

            mlp(0)
            for c in range(12):
                load(DIFF + c, cols(a["odd_in"], 256 * c))
            for c in range(4):
                load(DIFF + 12 + c, cols(a["odd_out"], 256 * c))
            mlp(1)
            dst, s = slot_of(POOL)
            d5 = dst.rearrange("p (g k n) -> p g k n", g=4, k=2)
            for g in range(4):
                sp.dma_start(d5[:, g], a["w_pool"][g].rearrange("(k p) n -> p k n", p=128)).then_inc(s, 16)
            mlp(2)
            for c in range(12):
                load(MOBA + c, cols(a["w_qkv"], 256 * c))
            for c in range(4):
                load(MOBA + 12 + c, cols(a["w_o"], 256 * c))
            mlp(3)
            for t in range(NT):
                sp.wait_ge(fin_act, t + 1)
                sp.wait_ge(fin_dve, t + 1)
                sp.dma_start(a["out"][128 * t:128 * t + 128, :], out2[:, t, :]).then_inc(out_done, 16)
            sp.wait_ge(out_done, 16 * NT)

        MORE = {1: 3, 2: 2, 6: 3, 7: 3, raw_index(POOL): 3}

        def loaded_value(n):
            return 16 * (n // RING + 1 + sum(x for c, x in MORE.items() if c <= n and c % RING == n % RING))

        @block.gpsimd
        def _(pool):
            pool.dma_start(relb, a["rel_bias"]).then_inc(in_misc, 16)
            pool.dma_start(hot, a["hot"]).then_inc(in_misc, 16)
            pool.dma_start(gmask, a["gmask"]).then_inc(in_misc, 16)
            pool.dma_start(lamw[:, :, :], a["lam"].partition_broadcast(128)).then_inc(in_misc, 16)
            for i, kv in enumerate((0, 0, 1)):
                pool.dma_start(w2[:, :, 64 * i:64 * i + 64],
                               a["cmp_w2"][kv].rearrange("(f p) n -> p f n", p=128)).then_inc(in_w2, 16)
            pool.wait_ge(bias_sb, 1)
            pool.dma_start(gdram, gb[:, :]).then_inc(bias_out, 16)
            pool.wait_ge(e_add, 5)
            pool.wait_ge(ul_ready, 8)
            for c in range(4):
                src = qk[64 * (c % 2):64 * (c % 2) + 64, KC + c // 2, :]
                pool.dma_start(kc2[0:64, c, :], src).then_inc(kc2_in, 16)
                pool.dma_start(kc2[64:128, c, 0:T - 1], src[:, 1:T]).then_inc(kc2_in, 16)

            def mod_rows(m, j, k):
                g = 2 * m + j
                return a["w_mod"][g // 3][bass.ds(k * 128, 128), 2048 * (g % 3):2048 * (g % 3) + 2048]

            for m in range(3):
                pool.wait_ge(acc_ready, acc_no((1, 3, 6)[m]) + 4)
                for j in range(2):
                    pool.dma_start(stage[j], mod_rows(m, j, 0)).then_inc(st_loaded[j], 16)
                with pool.Fori(1, KB) as k:
                    for j in range(2):
                        pool.wait_ge(st_done[j], k + KB * m)
                        pool.dma_start(stage[j], mod_rows(m, j, k)).then_inc(st_loaded[j], 16)
            pool.wait_ge(bias_out, 16)
            pool.wait_ge(ul_ready, ul_no(7) + 8)
            for h in range(16):
                if h >= 8:
                    pool.wait_ge(s_ps["b"], h - 7)
                row = gdram[h:h + 1, 0:T]
                pool.dma_start(hank[:, h % 8, :], bass.AP(row.tensor, row.offset, [[1, 128], [1, T]]))\
                    .then_inc(h_in[h % 8], 16)

        @block.scalar
        def _(act):
            split = [0]

            def hi_upto(m):
                while split[0] <= min(m, LAST - 1):
                    c = split[0]
                    n = raw_index(c)
                    act.wait_ge(loaded[n % RING], loaded_value(n))
                    if c >= RING:
                        act.wait_ge(used, c - RING + 1)
                    w = KB * 92 if c == 2 else SPLIT
                    nc.scalar.activation(whi[:, c % RING, 0:w], raw[:, n % RING, 0:w], ACT.Copy).then_inc(hi_ready, 1)
                    split[0] += 1

            def squares(e, j):
                act.wait_ge(x_ready, 4 * e + j + 1)
                nc.scalar.activation(u[:, 2 * j:2 * j + 2, :], xT[:, 2 * j:2 * j + 2, :], ACT.Square)\
                    .then_inc(sq_ready, 1)

            def norm(e, shift, out=None):
                act.wait_ge(rv_ready, e + 1)
                nc.scalar.activation(rstd[:, :], var[:, :], ACT.Sqrt).then_inc(rstd_ready, 1)
                if shift is None:
                    return
                for b in range(KB):
                    act.wait_ge(u_ready, u_no(e) + b + 1)
                    nc.scalar.activation(uh[:, b, :] if out is None else out[:, b, :], u[:, b, :],
                                         ACT.Identity, bias=shift[:, b:b + 1]).then_inc(uh_ready, 1)

            def mlp(l):
                m0 = MLPS[l]
                b = m0 % RING

                def relu(s, n):
                    act.wait_ge(used, n)
                    return nc.scalar.activation(work[:, s % 2, :], bank[s % 2][:, :], ACT.Relu)

                def upper(s, n):
                    act.wait_ge(h_done, n)
                    return nc.scalar.activation(hh[:, s % 2, :], work[:, 2 + s % 2, :], ACT.Copy)

                for s in range(3):
                    if s == 2:
                        act.wait_ge(h_done, 16 * l + 1)
                        hi_upto(m0 + 6)
                    relu(s, m0 + up_idx(s) + 1).then_inc(relu_done, 1)
                    hi_upto(m0 + (4, 5, 7)[s])
                    if s == 2:
                        act.wait_ge(used, m0 + dn_idx(0) + 1)
                    upper(s, 16 * l + s + 1).then_inc(hh_done, 1)
                with act.Fori(1, 7) as it:
                    for i in range(1, 5):
                        m = m0 + i + 3
                        n = raw_index(m)
                        if i % 2 == 0:
                            s = i // 2
                            act.wait_ge(h_done, it * 2 + (16 * l + s - 1))
                            relu(s, it * 4 + (m0 + 2 * s)).then_inc(relu_done, 1)
                        act.wait_ge(loaded[n % RING], it * 16 + loaded_value(n))
                        act.wait_ge(used, it * 4 + (m - RING + 1))
                        nc.scalar.activation(whi[:, m % RING, :], raw[:, n % RING, :], ACT.Copy).then_inc(hi_ready, 1)
                        if i % 2 == 0:
                            upper(s, it * 2 + (16 * l + s + 1)).then_inc(hh_done, 1)
                split[0] = m0 + 32
                hi_upto(m0 + 32)
                act.wait_ge(h_done, 16 * l + 14)
                relu(15, m0 + 30).then_inc(relu_done, 1)
                hi_upto(m0 + 33)
                upper(15, 16 * l + 16).then_inc(hh_done, 1)
                hi_upto(m0 + 34)

            def exps(ph, i, size):
                act.wait_ge(s_max[ph], i + 1)
                if i >= size:
                    act.wait_ge(s_tr[ph], (i - size) // (2 if ph == "d" else 1) + 1)
                b = bank[i % 3]
                nc.scalar.activation(P[:, i % size, 0:128], b[:, 0:128], ACT.Exp, bias=nmax[:, i, 0:1],
                                     accum_out=sums[:, i, 0:1])
                nc.scalar.activation(P[:, i % size, 128:384], b[:, 128:384], ACT.Exp, bias=nmax[:, i, 1:2],
                                     accum_out=sums[:, i, 1:2]).then_inc(s_exp[ph], 1)

            def out_upper(r, scale):
                for j in range(4):
                    act.wait_ge(oT_ready, 4 * r + j + 1)
                    nc.scalar.activation(uh[:, 2 * j:2 * j + 2, :],
                                         bank[j][:, :].rearrange("p (b n) -> p b n", b=2),
                                         ACT.Copy, scale=scale).then_inc(oh_ready, 1)

            r = 0
            for name, n in (("mix_g", 16), ("mlp_g", 16), ("fin_g", 8), ("mix_g2", 16), ("mlp_g2", 16),
                            ("fin_g2", 8), ("pool_s", 8), ("c", 8), ("sub_g", 1)):
                act.dma_start(rows[r:r + n, :], a[name].rearrange("(r n) -> r n", n=128)).then_inc(in_rows, 16)
                r += n
            act.dma_start(rows2[0:96, :], a["b_mod"].rearrange("(r n) -> r n", n=128)).then_inc(in_rows, 16)
            act.dma_start(rows2[96:128, :], a["cmp_pe"].rearrange("(r n) -> r n", n=128)).then_inc(in_rows, 16)
            for j in range(4):
                squares(0, j)
            hi_upto(0)
            norm(0, zero8)
            hi_upto(3)
            act.wait_ge(vec_ready, 1)
            nc.scalar.activation(cact[:, :], vec[:, V_C:V_C + 8], ACT.Exp, scale=-1.0).then_inc(vec_ready, 1)
            act.wait_ge(lam_in, 1)
            nc.scalar.activation(lam[:, 2:4], lam[:, 0:2], ACT.Exp).then_inc(lam_exp, 1)
            for i in range(10):
                if i == 3:
                    act.wait_ge(gate_in, 1)
                    nc.scalar.activation(gates[:, :, :], tk[:, :, 68:92], ACT.Exp, scale=-1.0).then_inc(gate_exp, 1)
                    for h in range(4):
                        act.wait_ge(e_is, h + 1)
                        nc.scalar.activation(P[:, h, :], bank[4 + h][:, 0:384], ACT.Relu).then_inc(e_ir, 1)
                hi_upto(min(EVEN + i + 4, PLAIN_AT - 1))
            act.wait_ge(e_sel, 1)
            for i in range(24):
                exps("e", i, 4)
                if i == 3:
                    act.wait_ge(plain_used, NPLAIN)
                    nc.scalar.activation(hact, bank[7][0:30, :], ACT.Square).then_inc(g_sq, 1)
                if i == 4:
                    act.wait_ge(g_in, 1)
                    nc.scalar.activation(hact, htmp, ACT.Tanh, scale=math.sqrt(2 / math.pi))\
                        .then_inc(g_th, 1)
                if i == 8:
                    act.wait_ge(sc_sub, 1)
                    nc.scalar.activation(pc[:, :, :], pc[:, :, :], ACT.Exp).then_inc(sc_exp, 1)
                if i in (6, 10, 14, 18):
                    hi_upto(10 + (i - 6) // 4)
            out_upper(0, one_col)
            for j in range(4):
                squares(1, j)
                if j < 3:
                    hi_upto(MLP0 + j)
            norm(1, zero8)
            hi_upto(MLP0 + 3)
            mlp(0)
            for j in range(4):
                squares(2, j)
            norm(2, zero8)
            hi_upto(DIFF + 3)
            for i in range(12):
                if i >= 8:
                    act.wait_ge(used, DIFF + i + 1)
                    c = i - 8
                    nc.scalar.activation(v_[:, :, 256 * c:256 * c + 256],
                                         bank[i % 2][:, :].rearrange("p (t n) -> p t n", t=NT), ACT.Copy)\
                        .then_inc(d_v, 1)
                hi_upto(DIFF + i + 4)
            for i in range(16):
                exps("d", i, 4)
            for t in range(NT):
                act.wait_ge(d_sq, t + 1)
                nc.scalar.activation(u[:, 4 * t:4 * t + 4, :], o_[:, t, :].rearrange("p (b n) -> p b n", b=4),
                                     ACT.Square).then_inc(d_rt, 1)
            act.wait_ge(d_rv, 1)
            nc.scalar.activation(msq[:, :, :], msq[:, :, :], ACT.Sqrt).then_inc(d_rt, 1)
            out_upper(1, lam[:, 6:7])
            for j in range(4):
                squares(3, j)
                if j < 3:
                    hi_upto(MLP1 + j)
            norm(3, zero8)
            hi_upto(MLP1 + 3)
            mlp(1)
            for j in range(4):
                squares(4, j)
            norm(4, None)
            for j in range(4):
                squares(5, j)
            norm(5, mod[:, 0:8], qk[:, 0:8, :])
            hi_upto(POOL + 3)
            for g in range(4):
                act.wait_ge(p_sum, g + 1)
                nc.scalar.activation(uh[:, 2 * g:2 * g + 2, :], u[:, 2 * g:2 * g + 2, :], ACT.Copy).then_inc(p_hi, 1)
            for j in range(4):
                squares(6, j)
            norm(6, mod[:, 24:32])
            hi_upto(MLP2 + 3)
            mlp(2)
            for j in range(4):
                squares(7, j)
            norm(7, mod[:, 48:56])
            hi_upto(MOBA + 3)
            for i in range(12):
                act.wait_ge(used, MOBA + i + 1)
                b = bank[i % 2][:, :].rearrange("p (t n) -> p t n", t=2)
                if i < 4:
                    nc.scalar.activation(qk[:, 2 * i:2 * i + 2, :], b, ACT.Copy, scale=HD ** -0.5).then_inc(b_copied, 1)
                elif i < 8:
                    nc.scalar.activation(qk[:, 2 * i:2 * i + 2, :], b, ACT.Copy).then_inc(b_copied, 1)
                else:
                    c = i - 8
                    nc.scalar.activation(v_[:, :, 256 * c:256 * c + 256], b, ACT.Copy).then_inc(b_copied, 1)
                hi_upto(MOBA + i + 4)
            for i in range(16):
                exps("b", i, 4)
            out_upper(2, one_col)
            for j in range(4):
                squares(8, j)
                if j < 3:
                    hi_upto(MLP3 + j)
            norm(8, mod[:, 72:80])
            hi_upto(MLP3 + 3)
            mlp(3)
            for j in range(4):
                squares(9, j)
            norm(9, None)
            for t in range(NT):
                act.wait_ge(fin_T, 2 * t + 1)
                nc.scalar.activation(out2[:, t, 0:512], bank[4 + 2 * t][:, :], ACT.Copy).then_inc(fin_act, 1)

        @block.vector
        def _(dve):
            split = [0]
            chain = [0]

            def link(ins):
                chain[0] += 1
                ins.then_inc(dchain, 1)
                dve.wait_ge(dchain, chain[0])

            def lower(m, n, w=SPLIT):
                return nc.vector.tensor_tensor(wlo[:, m % RING, 0:w], raw[:, n % RING, 0:w],
                                               whi[:, m % RING, 0:w].bitcast(fp32), ALU.subtract)

            def lo_upto(m):
                while split[0] <= min(m, LAST - 1):
                    c = split[0]
                    dve.wait_ge(hi_ready, c + 1)
                    lower(c, raw_index(c), KB * 92 if c == 2 else SPLIT).then_inc(lo_ready, 1)
                    split[0] += 1

            def residual(e, j, gate):
                dve.wait_ge(acc_ready, acc_no(e) + j + 1)
                for b in (2 * j, 2 * j + 1):
                    ins = nc.vector.scalar_tensor_tensor(
                        out=xT[:, b, :], in0=bank[4 + j][:, 256 * (b % 2):256 * (b % 2) + 256], scalar=gate[:, b:b + 1],
                        in1=xT[:, b, :], op0=ALU.mult, op1=ALU.add)
                ins.then_inc(x_ready, 1)

            def inv_var(e):
                dve.wait_ge(sumsq_ready, e + 1)
                link(nc.vector.tensor_scalar(var[:, :], bank[2][:, 0:T], 1.0 / D, EPS, ALU.mult, ALU.add))
                nc.vector.reciprocal(var[:, :], var[:, :]).then_inc(rv_ready, 1)
                dve.wait_ge(rstd_ready, e + 1)

            def normed(out, g, b):
                return nc.vector.scalar_tensor_tensor(out=out[:, b, :], in0=xT[:, b, :], scalar=g[:, b:b + 1],
                                                      in1=rstd[:, :], op0=ALU.mult, op1=ALU.mult)

            def norm(e, g, shift):
                inv_var(e)

                def low(b):
                    dve.wait_ge(uh_ready, u_no(e) + b + 1)
                    nc.vector.scalar_tensor_tensor(out=ul[:, b, :], in0=u[:, b, :], scalar=shift[:, b:b + 1],
                                                   in1=uh[:, b, :].bitcast(fp32), op0=ALU.add, op1=ALU.subtract)\
                        .then_inc(ul_ready, 1)

                for b in range(KB):
                    normed(u, g, b).then_inc(u_ready, 1)
                    if b >= 1:
                        low(b - 1)
                low(KB - 1)

            def mlp(l):
                m0 = MLPS[l]

                def square(s, n):
                    dve.wait_ge(relu_done, n)
                    return nc.vector.tensor_tensor(work[:, 2 + s % 2, :], work[:, s % 2, :], work[:, s % 2, :], ALU.mult)

                def low(s, n):
                    dve.wait_ge(hh_done, n)
                    dve.wait_ge(h_done, n)
                    return nc.vector.tensor_tensor(hl[:, s % 2, :], work[:, 2 + s % 2, :],
                                                   hh[:, s % 2, :].bitcast(fp32), ALU.subtract)

                def add_rows(j, k, n):
                    dve.wait_ge(st_loaded[j], n)
                    if isinstance(k, int) and k == 0:
                        return nc.vector.tensor_scalar(acc[j], stage[j], cact[:, 0:1], None, ALU.mult)
                    return nc.vector.scalar_tensor_tensor(out=acc[j], in0=stage[j],
                                                          scalar=cact[:, k:k + 1] if isinstance(k, int)
                                                          else cact[:, bass.ds(k, 1)],
                                                          in1=acc[j], op0=ALU.mult, op1=ALU.add)

                for s in range(3):
                    if s == 2:
                        lo_upto(m0 + 6)
                        if l < 3:
                            add_rows(1, 0, 16 * (KB * l + 1)).then_inc(st_done[1], 1)
                    if s == 2:
                        dve.wait_ge(hh_done, 16 * l + 1)
                        dve.wait_ge(hl_done, 16 * l + 1)
                    square(s, 16 * l + s + 1).then_inc(h_done, 1)
                    lo_upto(m0 + (4, 5, 7)[s])
                    low(s, 16 * l + s + 1).then_inc(hl_done, 1)
                    if s == 0 and l < 3:
                        add_rows(0, 0, 16 * (KB * l + 1)).then_inc(st_done[0], 1)
                with dve.Fori(1, 7) as it:
                    for i in range(1, 5):
                        m = m0 + i + 3
                        n = raw_index(m)
                        if i % 2 == 0:
                            s = i // 2
                            dve.wait_ge(hh_done, it * 2 + (16 * l + s - 1))
                            dve.wait_ge(hl_done, it * 2 + (16 * l + s - 1))
                            square(s, it * 2 + (16 * l + s + 1)).then_inc(h_done, 1)
                        dve.wait_ge(hi_ready, it * 4 + (m + 1))
                        lower(m, n).then_inc(lo_ready, 1)
                        if i % 2 == 0:
                            low(s, it * 2 + (16 * l + s + 1)).then_inc(hl_done, 1)
                        elif l < 3:
                            j = i // 2
                            dve.wait_ge(st_done[j], it + KB * l)
                            add_rows(j, it, it * 16 + 16 * (KB * l + 1)).then_inc(st_done[j], 1)
                split[0] = m0 + 32
                lo_upto(m0 + 32)
                if l < 3:
                    dve.wait_ge(st_done[0], KB * l + 7)
                    add_rows(0, 7, 16 * (KB * l + 8)).then_inc(st_done[0], 1)
                dve.wait_ge(hh_done, 16 * l + 14)
                dve.wait_ge(hl_done, 16 * l + 14)
                square(15, 16 * l + 16).then_inc(h_done, 1)
                lo_upto(m0 + 33)
                low(15, 16 * l + 16).then_inc(hl_done, 1)
                lo_upto(m0 + 34)
                if l < 3:
                    dve.wait_ge(st_done[1], KB * l + 7)
                    add_rows(1, 7, 16 * (KB * l + 8)).then_inc(st_done[1], 1)

            def mod_vectors(m):
                dve.wait_ge(mod_T, m + 1)
                link(nc.vector.tensor_tensor(mod[:, 32 * m:32 * m + 32], bank[3][:, 0:32],
                                             bpe[:, 32 * m:32 * m + 32], ALU.add))

                def scaled(i, sc, g):
                    return nc.vector.scalar_tensor_tensor(out=gain[:, i, :], in0=mod[:, sc:sc + 8], scalar=1.0,
                                                          in1=vec[:, g:g + 8], op0=ALU.add, op1=ALU.mult)
                if m == 0:
                    scaled(0, 8, V_MIX2)
                    ins = nc.vector.tensor_tensor(gpool[:, :], mod[:, 16:24], vec[:, V_POOL:V_POOL + 8], ALU.mult)
                elif m == 1:
                    scaled(1, 32, V_MLP2)
                    ins = scaled(2, 56, V_MIX2 + 8)
                else:
                    ins = scaled(3, 80, V_MLP2 + 8)
                ins.then_inc(mod_ready, 1)
                dve.wait_ge(mod_ready, m + 1)

            def maxima(ph, i):
                dve.wait_ge(s_ps[ph], i + 1)
                b = bank[i % 3]
                nc.vector.tensor_reduce(nmax[:, i, 0:1], b[:, 0:128], AX.X, ALU.max, negate=True)
                nc.vector.tensor_reduce(nmax[:, i, 1:2], b[:, 128:384], AX.X, ALU.max, negate=True)\
                    .then_inc(s_max[ph], 1)

            def evac(ph, i):
                dve.wait_ge(s_tr[ph], i + 1)
                if i >= 2:
                    dve.wait_ge(s_pv[ph], i - 1)
                nc.vector.tensor_copy(PT[:, i % 2, :], bank[3][:, 0:384]).then_inc(s_pt[ph], 1)

            def out_lower(r, scale):
                for j in range(4):
                    dve.wait_ge(oh_ready, 4 * r + j + 1)
                    nc.vector.scalar_tensor_tensor(
                        out=ul[:, 2 * j:2 * j + 2, :], in0=bank[j][:, :].rearrange("p (b n) -> p b n", b=2),
                        scalar=scale, in1=uh[:, 2 * j:2 * j + 2, :].bitcast(fp32), op0=ALU.mult, op1=ALU.subtract)\
                        .then_inc(ol_ready, 1)

            def rope_parts(b, n, q, r):
                cs = con[:, (C_COSQ if q else C_COS):][:, 0:T].unsqueeze(1).to_broadcast([128, n, T])
                sn = con[:, (C_SINQ if q else C_SIN):][:, 0:T].unsqueeze(1).to_broadcast([128, n, T])
                src = b[:, 0:256 * n].rearrange("p (b n) -> p b n", b=n)
                t1 = work[:, r % 2, 0:256 * n].rearrange("p (b n) -> p b n", b=n)
                t2 = work[:, 2 + r % 2, 0:256 * n].rearrange("p (b n) -> p b n", b=n)
                nc.vector.tensor_tensor(t1, src, cs, ALU.mult)
                return nc.vector.tensor_tensor(t2, src, sn, ALU.mult)

            def rope_sum(dst, n, r):
                return nc.vector.tensor_tensor(dst, bank[2 + r % 2][:, 0:256 * n].rearrange("p (b n) -> p b n", b=n),
                                               work[:, r % 2, 0:256 * n].rearrange("p (b n) -> p b n", b=n), ALU.add)

            nc.vector.memset(ones[:, :], 1.0)
            nc.vector.memset(zero8[:, :], 0.0)
            nc.vector.memset(xT[:, :, :], 0.0).then_inc(zeroed, 1)
            dve.wait_ge(in_con, 16)
            nc.vector.tensor_copy(idb[:, :], ident)
            nc.vector.tensor_scalar(trib[:, :], tri, -1.0, -NEG, ALU.max, ALU.mult).then_inc(zeroed, 1)
            dve.wait_ge(zeroed, 2)
            for j in range(4):
                residual(0, j, ones)
            dve.wait_ge(vec_T, 1)
            nc.vector.tensor_copy(vec[:, :], bank[0][:, 0:NV])
            nc.vector.tensor_copy(bpe[:, :], bank[1][:, 0:128]).then_inc(vec_ready, 1)
            lo_upto(0)
            norm(0, vec[:, V_MIX:], zero8)
            lo_upto(3)
            dve.wait_ge(in_misc, 64)
            for i in range(2):
                ins = nc.vector.tensor_tensor(lamp[:, i, :], lamw[:, 2 * i, :], lamw[:, 2 * i + 1, :], ALU.mult)
            link(ins)
            nc.vector.tensor_reduce(lam[:, 0:2], lamp[:, :, :], AX.X, ALU.add).then_inc(lam_in, 1)
            dve.wait_ge(vec_ready, 2)
            link(nc.vector.tensor_scalar(cact[:, :], cact[:, :], 1.0, None, ALU.add))
            link(nc.vector.reciprocal(cact[:, :], cact[:, :]))
            link(nc.vector.tensor_tensor(cact[:, :], cact[:, :], vec[:, V_C:V_C + 8], ALU.mult))
            dve.wait_ge(lam_exp, 1)
            link(nc.vector.tensor_tensor(lam[:, 4:5], lam[:, 3:4], lam[:, 2:3], ALU.subtract))
            link(nc.vector.tensor_scalar(lam[:, 5:6], lam[:, 4:5], -LAM_INIT, None, ALU.add))
            link(nc.vector.tensor_scalar(lam[:, 6:7], vec[:, V_SUB:V_SUB + 1], 1.0 - LAM_INIT, None, ALU.mult))
            dve.wait_ge(bias_T, 1)
            nc.vector.tensor_tensor(gb[:, :], bank[3][0:16, 0:384], gmask, ALU.add).then_inc(bias_sb, 1)

            dve.wait_ge(bias_sb, 1)
            ROPE = {0: (2, QI, True), 1: (2, KA, False), 3: (2, QA, True), 4: (2, QA + 2, True), 5: (1, KC, False),
                    6: (2, QB, True), 7: (2, QB + 2, True), 8: (1, KS, False), 9: (1, KW, False)}
            order = [0, 1, 3, 4, 5, 6, 7, 8, 9]
            wide = score[:, :]
            parts = ((0, 128), (128, 384))

            def index_scores():
                for h in range(4):
                    dve.wait_ge(e_ir, h + 1)
                    for t, (c0, c1) in enumerate(parts):
                        if h == 0:
                            ins = nc.vector.tensor_scalar(score[:, c0:c1], P[:, 0, c0:c1], tk[:, t, 64:65], None, ALU.mult)
                        else:
                            ins = nc.vector.scalar_tensor_tensor(out=score[:, c0:c1], in0=P[:, h, c0:c1],
                                                                 scalar=tk[:, t, 64 + h:65 + h], in1=score[:, c0:c1],
                                                                 op0=ALU.mult, op1=ALU.add)
                    link(ins)
                for c0 in (0, 256):
                    ins = nc.vector.tensor_tensor(score[:, c0:c0 + 128], score[:, c0:c0 + 128], tri, ALU.add)
                link(ins)

            def take8(n):
                for _ in range(n):
                    for t, (c0, c1) in enumerate(parts):
                        ins = nc.vector.max(top8[:, t, :], score[:, c0:c1])
                    link(ins)
                    for t, (c0, c1) in enumerate(parts):
                        ins = nc.vector.match_replace(score[:, c0:c1], top8[:, t, :], score[:, c0:c1], MARK)
                    link(ins)

            for i in range(10):
                if i == 9:
                    dve.wait_ge(kc2_in, 128)
                    for c in range(4):
                        kv, g = c // 2, c % 2
                        src = bass.AP(kc2.tensor, kc2.offset + c * T, [list(kc2.ap[0]), [2, 16], [16, NBLK]])
                        ins = nc.vector.tensor_tensor(blk[:, kv, :, NBLK * g:NBLK * g + NBLK], src,
                                                      bpe[:, 96 + 16 * kv:112 + 16 * kv].unsqueeze(2).to_broadcast([128, 16, NBLK]),
                                                      ALU.add)
                    ins.then_inc(blk_ready, 1)
                dve.wait_ge(used, EVEN + i + 1)
                if i in ROPE:
                    n, b0, q = ROPE[i]
                    r = order.index(i)
                    if n == 1:
                        if i == 5:
                            nc.vector.tensor_copy(qk[:, VC, :], bank[i % 2][:, 256:512])
                        else:
                            c = 128 * (i - 8)
                            nc.vector.tensor_copy(v_[:, :, c:c + 128],
                                                  bank[i % 2][:, 256:512].rearrange("p (t n) -> p t n", t=NT))
                    if r >= 2:
                        dve.wait_ge(e_add, r - 1)
                    rope_parts(bank[i % 2], n, q, r).then_inc(e_t2, 1)
                else:
                    nc.vector.tensor_copy(tk[:, :, :], bank[i % 2][:, 0:NT * 92].rearrange("p (t n) -> p t n", t=NT))\
                        .then_inc(gate_in, 1)
                lo_upto(min(EVEN + i + 4, PLAIN_AT - 1))
                if i in ROPE:
                    dve.wait_ge(e_sw, r + 1)
                    rope_sum(qk[:, b0:b0 + n, :], n, r).then_inc(e_add, 1)
                if i == 3:
                    index_scores()
                if 4 <= i < 8:
                    take8(2)
            nc.vector.tensor_scalar(sel[:, :], wide, MARK, NEG, ALU.not_equal, ALU.mult).then_inc(e_sel, 1)
            dve.wait_ge(gate_exp, 1)
            link(nc.vector.tensor_scalar(gates[:, :, :], gates[:, :, :], 1.0, None, ALU.add))
            link(nc.vector.reciprocal(gates[:, :, :], gates[:, :, :]))
            def gelu_in():
                dve.wait_ge(g_sq, 1)
                link(nc.vector.tensor_scalar(htmp, hact, 0.044715, 1.0, ALU.mult, ALU.add))
                nc.vector.tensor_tensor(htmp, bank[7][0:30, :], htmp, ALU.mult).then_inc(g_in, 1)

            def gelu():
                dve.wait_ge(g_th, 1)
                link(nc.vector.tensor_scalar(hact, hact, 1.0, 0.5, ALU.add, ALU.mult))
                nc.vector.tensor_tensor(hact, bank[7][0:30, :], hact, ALU.mult).then_inc(h_act, 1)

            def hidden():
                dve.wait_ge(hT_ps, 1)
                nc.vector.tensor_copy(hT[:, :, :].rearrange("p c n -> p (c n)"), bank[6][:, 256:376])
                for f in range(2):
                    for g in range(2):
                        c = 256 + 30 * (2 + f) + NBLK * g
                        ins = nc.vector.tensor_copy(
                            hrep[:, f, 60 * g:60 * g + 60].rearrange("p (j n) -> p j n", j=4),
                            bank[6][:, c:c + NBLK].unsqueeze(1).to_broadcast([128, 4, NBLK]))
                ins.then_inc(hT_ready, 1)

            def compressed_keys():
                dve.wait_ge(kv_ps, 1)
                nc.vector.tensor_copy(kcm[:, :], bank[6][:, 0:30])
                nc.vector.tensor_tensor(vbd[0:CW, :, :], bank[6][0:CW, 64:128].unsqueeze(1).to_broadcast([CW, 8, HD]),
                                        con[0:CW, C_HB:C_HB + 8].unsqueeze(2).to_broadcast([CW, 8, HD]), ALU.mult)\
                    .then_inc(kv_ready, 1)

            def compressed_scores():
                dve.wait_ge(sc_ps, 1)
                for t in range(NT):
                    cm = con[:, C_CMP + NBLK * t:C_CMP + NBLK * t + NBLK].unsqueeze(1).to_broadcast([128, 8, NBLK])
                    pt3 = pc[:, t, :].rearrange("p (h n) -> p h n", h=8)
                    link(nc.vector.tensor_scalar(gtmp[:, t, 0:CW].rearrange("p (h n) -> p h n", h=8), cm, 1.0, -NEG,
                                                 ALU.subtract, ALU.mult))
                    for g in range(2):
                        c = slice(4 * NBLK * g, 4 * NBLK * g + 4 * NBLK)
                        ins = nc.vector.tensor_tensor(pc[:, t, c], bank[6 + g][:, 128 + 4 * NBLK * t:128 + 4 * NBLK * t + 4 * NBLK],
                                                      gtmp[:, t, c], ALU.add)
                    link(ins)
                    link(nc.vector.tensor_reduce(cst[:, 0, 8 * t:8 * t + 8], pt3, AX.X, ALU.max))
                    ins = nc.vector.tensor_tensor(pt3, pt3, cst[:, 0, 8 * t:8 * t + 8].unsqueeze(2).to_broadcast([128, 8, NBLK]),
                                                  ALU.subtract)
                ins.then_inc(sc_sub, 1)

            def compressed_softmax():
                dve.wait_ge(sc_exp, 1)
                for t in range(NT):
                    cm = con[:, C_CMP + NBLK * t:C_CMP + NBLK * t + NBLK].unsqueeze(1).to_broadcast([128, 8, NBLK])
                    pt3 = pc[:, t, :].rearrange("p (h n) -> p h n", h=8)
                    link(nc.vector.tensor_tensor(pt3, pt3, cm, ALU.mult))
                    link(nc.vector.tensor_reduce(cst[:, 1, 8 * t:8 * t + 8], pt3, AX.X, ALU.add))
                    link(nc.vector.tensor_scalar(cst[:, 2, 8 * t:8 * t + 8], cst[:, 1, 8 * t:8 * t + 8], 1e-30, None, ALU.max))
                    link(nc.vector.reciprocal(cst[:, 3, 8 * t:8 * t + 8], cst[:, 2, 8 * t:8 * t + 8]))
                    link(nc.vector.tensor_tensor(cst[:, 4, 8 * t:8 * t + 8], cst[:, 3, 8 * t:8 * t + 8],
                                                 gates[:, t, :].rearrange("p (h c) -> p h c", c=3)[:, :, 0], ALU.mult))
                    nc.vector.tensor_tensor(pt3, pt3, cst[:, 4, 8 * t:8 * t + 8].unsqueeze(2).to_broadcast([128, 8, NBLK]),
                                            ALU.mult).then_inc(pc_ready, 1)

            def even_out(kind):
                dve.wait_ge(s_pv["e"], 8 * kind + 8)
                dve.wait_ge(s_exp["e"], 8 * kind + 8)
                k8 = slice(8 * kind, 8 * kind + 8)
                link(nc.vector.reciprocal(rs[:, k8, :], sums[:, k8, :]))
                for t in range(NT):
                    if kind:
                        link(nc.vector.tensor_tensor(rs[:, k8, t], rs[:, k8, t],
                                                     gates[:, t, :].rearrange("p (h c) -> p h c", c=3)[:, :, kind], ALU.mult))
                    f = rs[:, k8, t].unsqueeze(2).to_broadcast([128, 8, HD])
                    src = bank[(4, 6, 4)[kind] + t][:, :].rearrange("p (h n) -> p h n", h=8)
                    oo = o_[:, t, (0 if kind == 0 else 512):][:, 0:512].rearrange("p (h n) -> p h n", h=8)
                    if kind < 2:
                        ins = nc.vector.tensor_tensor(oo, src, f, ALU.mult)
                    else:
                        tmp = work[:, t, :].rearrange("p (h n) -> p h n", h=8)
                        link(nc.vector.tensor_tensor(tmp, src, f, ALU.mult))
                        dve.wait_ge(o_free, 3)
                        nc.vector.tensor_tensor(oo, oo, tmp, ALU.add).then_inc(o_ready, 1)
                if kind < 2:
                    ins.then_inc(o_free, 1)

            dve.wait_ge(bias_out, 16)
            for i in range(24 + 2):
                if i < 24:
                    maxima("e", i)
                if i >= 2:
                    evac("e", i - 2)
                if i == 4:
                    gelu_in()
                    gelu()
                if i == 5:
                    hidden()
                if i == 6:
                    compressed_keys()
                if i == 7:
                    compressed_scores()
                if i == 9:
                    compressed_softmax()
                if i == 11:
                    for t in range(NT):
                        dve.wait_ge(pc_ps, t + 1)
                        nc.vector.tensor_copy(pcT[0:CW, t, :], bank[3][0:CW, 384:512]).then_inc(pcT_ready, 1)
                if i in (6, 10, 14, 18):
                    lo_upto(10 + (i - 6) // 4)
                if i in (12, 20):
                    even_out(i // 8 - 1)
                if i == 24:
                    dve.wait_ge(oc_ps, 1)
                    dve.wait_ge(o_free, 2)
                    for t in range(NT):
                        ins = nc.vector.tensor_tensor(o_[:, t, 512:1024], o_[:, t, 512:1024], bank[6 + t][:, :], ALU.add)
                    ins.then_inc(o_free, 1)
            even_out(2)
            out_lower(0, one_col)

            def residuals(e, gate, split_to=None):
                for j in range(4):
                    residual(e, j, gate)
                    if split_to is not None and j < 3:
                        lo_upto(split_to + j)

            residuals(1, ones, MLP0)
            norm(1, vec[:, V_MLP:], zero8)
            lo_upto(MLP0 + 3)
            mlp(0)
            residuals(2, ones)
            norm(2, vec[:, V_MIX + 8:], zero8)
            lo_upto(DIFF + 3)
            mod_vectors(0)
            for i in range(12):
                if i < 8:
                    dve.wait_ge(used, DIFF + i + 1)
                    if i >= 2:
                        dve.wait_ge(d_add, i - 1)
                    rope_parts(bank[i % 2], 2, i < 4, i).then_inc(d_t2, 1)
                lo_upto(DIFF + i + 4)
                if i < 8:
                    dve.wait_ge(d_sw, i + 1)
                    rope_sum(qk[:, 2 * i:2 * i + 2, :], 2, i).then_inc(d_add, 1)

            def combine(i):
                dve.wait_ge(s_exp["d"], 2 * i + 2)
                link(nc.vector.reciprocal(rs[:, 2 * i, :], sums[:, 2 * i + 1, :]))
                link(nc.vector.scalar_tensor_tensor(out=rs[:, 2 * i + 1, :], in0=rs[:, 2 * i, :], scalar=lam[:, 5:6],
                                                    in1=sums[:, 2 * i, :], op0=ALU.mult, op1=ALU.mult))
                p0, p1 = 2 * i % 4, (2 * i + 1) % 4
                for t, (c0, c1) in enumerate(parts):
                    ins = nc.vector.scalar_tensor_tensor(out=P[:, p0, c0:c1], in0=P[:, p1, c0:c1],
                                                         scalar=rs[:, 2 * i + 1, t:t + 1], in1=P[:, p0, c0:c1],
                                                         op0=ALU.mult, op1=ALU.add)
                ins.then_inc(s_cmb, 1)

            for i in range(8 + 2):
                if i >= 2:
                    evac("d", i - 2)
                if 1 <= i <= 8:
                    combine(i - 1)
                if i < 8:
                    maxima("d", 2 * i)
                    maxima("d", 2 * i + 1)
            dve.wait_ge(s_pv["d"], 8)
            link(nc.vector.reciprocal(rs[:, 0:16, :], sums[:, 0:16, :]))
            for t in range(NT):
                for c in range(2):
                    ins = nc.vector.tensor_tensor(
                        o_[:, t, 512 * c:512 * c + 512].rearrange("p (h n) -> p h n", h=4),
                        bank[4 + 2 * t + c][:, :].rearrange("p (h n) -> p h n", h=4),
                        rs[:, 8 * c:8 * c + 8:2, t].unsqueeze(2).to_broadcast([128, 4, 128]), ALU.mult)
                ins.then_inc(d_sq, 1)
            for t in range(NT):
                dve.wait_ge(d_rt, t + 1)
                ins = nc.vector.tensor_reduce(msq[:, t, :], uf[:, 1024 * t:1024 * t + 1024].rearrange("p (h n) -> p h n", h=8),
                                              AX.X, ALU.add)
            link(ins)
            link(nc.vector.tensor_scalar(msq[:, :, :], msq[:, :, :], 1.0 / 128, EPS, ALU.mult, ALU.add))
            nc.vector.reciprocal(msq[:, :, :], msq[:, :, :]).then_inc(d_rv, 1)
            dve.wait_ge(d_rt, NT + 1)
            for t in range(NT):
                ot = o_[:, t, :].rearrange("p (h n) -> p h n", h=8)
                nc.vector.tensor_tensor(ot, ot, msq[:, t, :].unsqueeze(2).to_broadcast([128, 8, 128]), ALU.mult)\
                    .then_inc(o_ready, 1)
            out_lower(1, lam[:, 6:7])
            residuals(3, ones, MLP1)
            norm(3, vec[:, V_MLP + 8:], zero8)
            lo_upto(MLP1 + 3)
            mlp(1)
            residuals(4, ones)
            inv_var(4)
            for b in range(KB):
                ins = normed(xT, vec[:, V_FIN:], b)
                if b % 2:
                    ins.then_inc(x_ready, 1)
            dve.wait_ge(x_ready, 4 * 5 + 4)
            inv_var(5)
            for b in range(KB):
                normed(u, gain[:, 0, :], b).then_inc(u_ready, 1)
            hb, sa = qk[:, 0:8, :], qk[:, 8:16, :]
            sbb = P[:, :, :].rearrange("p a n -> p (a n)").rearrange("p (b n) -> p b n", n=T)
            dve.wait_ge(uh_ready, u_no(5) + 8)
            for g, w in enumerate((1, 2, 4, 8)):
                n = 8 - 2 * g
                src = (hb, sa[:, 2:8, :], sbb[:, 2:6, :], sa[:, 6:8, :])[g]
                dst = (sa, sbb, sa[:, 4:8, :], sbb[:, 4:6, :])[g]
                nc.vector.tensor_copy(dst[:, 0:n, 0:w], src[:, 0:n, 0:w])
                link(nc.vector.tensor_tensor(dst[:, 0:n, w:T], src[:, 0:n, w:T], src[:, 0:n, 0:T - w], ALU.add))
                cor = con[:, C_CORR + 32 * g:C_CORR + 32 * g + 32].rearrange("p (b n) -> p b n", b=2)
                link(nc.vector.tensor_tensor(dst[:, 0:2, 0:16], dst[:, 0:2, 0:16], cor, ALU.mult))
                nc.vector.scalar_tensor_tensor(out=u[:, 2 * g:2 * g + 2, :], in0=dst[:, 0:2, :],
                                               scalar=1.0 / (2 << g), in1=hb[:, 2 * g:2 * g + 2, :],
                                               op0=ALU.mult, op1=ALU.subtract).then_inc(p_sum, 1)
                if g:
                    dve.wait_ge(p_hi, g)
                    nc.vector.tensor_tensor(ul[:, 2 * g - 2:2 * g, :], u[:, 2 * g - 2:2 * g, :],
                                            uh[:, 2 * g - 2:2 * g, :].bitcast(fp32), ALU.subtract).then_inc(p_h, 1)
            dve.wait_ge(p_hi, 4)
            nc.vector.tensor_tensor(ul[:, 6:8, :], u[:, 6:8, :], uh[:, 6:8, :].bitcast(fp32), ALU.subtract).then_inc(p_h, 1)
            lo_upto(POOL + 3)
            mod_vectors(1)
            residuals(6, gpool)
            norm(6, gain[:, 1, :], mod[:, 24:32])
            lo_upto(MLP2 + 3)
            mlp(2)
            residuals(7, mod[:, 40:48])
            norm(7, gain[:, 2, :], mod[:, 48:56])
            lo_upto(MOBA + 3)
            mod_vectors(2)
            for i in range(12):
                lo_upto(MOBA + i + 4)
            for i in range(16 + 2):
                if i < 16:
                    maxima("b", i)
                if i >= 2:
                    evac("b", i - 2)
            dve.wait_ge(s_pv["b"], 16)
            link(nc.vector.reciprocal(rs[:, 0:16, :], sums[:, 0:16, :]))
            for t in range(NT):
                for c in range(2):
                    ins = nc.vector.tensor_tensor(
                        o_[:, t, 512 * c:512 * c + 512].rearrange("p (h n) -> p h n", h=8),
                        bank[4 + 2 * t + c][:, :].rearrange("p (h n) -> p h n", h=8),
                        rs[:, 8 * c:8 * c + 8, t].unsqueeze(2).to_broadcast([128, 8, HD]), ALU.mult)
                ins.then_inc(o_ready, 1)
            out_lower(2, one_col)
            residuals(8, mod[:, 64:72], MLP3)
            norm(8, gain[:, 3, :], mod[:, 72:80])
            lo_upto(MLP3 + 3)
            mlp(3)
            residuals(9, mod[:, 88:96])
            inv_var(9)
            for b in range(KB):
                normed(u, vec[:, V_FIN2:], b).then_inc(u_ready, 1)
            for t in range(NT):
                dve.wait_ge(fin_T, 2 * t + 2)
                nc.vector.tensor_copy(out2[:, t, 512:1024], bank[5 + 2 * t][:, :]).then_inc(fin_dve, 1)

        @block.tensor
        def _(pe):
            mm = nc.tensor.matmul

            def three(out, w_first, wh, wl, xh, xl, start, stop):
                for i, (wa, xa) in enumerate(((wh, xh), (wh, xl), (wl, xh))):
                    st, mv = (wa, xa) if w_first else (xa, wa)
                    ins = mm(out, st, mv, start=start and i == 0, stop=stop and i == 2, skip_group_check=True)
                return ins

            def weights(m, k=KB):
                r = m % RING
                return (whi[:, r, :].rearrange("p (k n) -> p k n", k=k), wlo[:, r, :].rearrange("p (k n) -> p k n", k=k))

            def features(m, out, sems=None, blocks=2):
                wh, wl = weights(m)
                for k in range(KB):
                    if sems is not None:
                        s, base, per = sems
                        pe.wait_ge(s, base + k // per + 1)
                    for b in range(blocks):
                        c = slice(128 * b, 128 * b + 128)
                        ins = three(out[:, 256 * b:256 * b + 256], True, wh[:, k, c], wl[:, k, c], uh[:, k, :], ul[:, k, :],
                                    k == 0 and b == 0, k == KB - 1)
                return ins

            def tokens(m, out, c0, n, o0=0, width=None, w=None):
                wh, wl = weights(m) if w is None else w
                for t in range(NT):
                    for k in range(KB):
                        ts = slice(128 * t, 128 * t + 128)
                        ins = three(out[:, o0 + n * t:o0 + n * t + n], False, wh[:, k, c0:c0 + n], wl[:, k, c0:c0 + n],
                                    uh[:, k, ts], ul[:, k, ts], t == 0 and k == 0 and o0 == 0, k == KB - 1)
                return ins

            def slot_free():
                mm(bank[3][0:1, 508:509], one_col, one_col, start=True, stop=True).then_inc(used, 1)

            def sumsq(e, j):
                pe.wait_ge(sq_ready, 4 * e + j + 1)
                for b in (2 * j, 2 * j + 1):
                    ins = mm(bank[2][:, 0:T], ones[:, :], u[:, b, :], start=b == 0, stop=b == KB - 1)
                if j == 3:
                    ins.then_inc(sumsq_ready, 1)

            def mod_sums(l, c0, c1):
                for j in range(2):
                    for c in range(max(c0, 16 * j), min(c1, 16 * j + 16)):
                        if c % 16 == 0:
                            pe.wait_ge(st_done[j], KB * (l + 1))
                        t = c % 16
                        ins = mm(bank[3][:, c:c + 1], acc[j][:, 128 * t:128 * t + 128], one_col, start=True, stop=True)
                if c1 == 32:
                    ins.then_inc(mod_T, 1)

            def mlp(l):
                m0 = MLPS[l]
                e = EVENT_OF_MLP[l]

                def up(s, m, first=False):
                    return features(m, bank[s % 2], (ul_ready, ul_no(e - 1), 1) if first else None)

                def down(s, m, first=False, last=False):
                    wh, wl = weights(m, 2)
                    for b in range(KB):
                        for k in range(2):
                            c = slice(128 * b, 128 * b + 128)
                            hs = slice(256 * k, 256 * k + 256)
                            ins = three(bank[4 + b // 2][:, 256 * (b % 2):256 * (b % 2) + 256], True, wh[:, k, c], wl[:, k, c],
                                        hh[:, s % 2, hs], hl[:, s % 2, hs], first and k == 0 and b % 2 == 0, last and k == 1)
                        if last and b % 2:
                            ins.then_inc(acc_ready, 1)
                            if b == KB - 1:
                                slot_free()
                            if b >= 5:
                                sumsq(e, (b - 5) // 2)
                    return ins

                pe.wait_ge(lo_ready, m0 + 1)
                up(0, m0, True).then_inc(used, 1)
                pe.wait_ge(lo_ready, m0 + 2)
                up(1, m0 + 1).then_inc(used, 1)
                pe.wait_ge(lo_ready, m0 + 3)
                pe.wait_ge(hl_done, 16 * l + 1)
                down(0, m0 + 2, first=True).then_inc(used, 1)
                pe.wait_ge(lo_ready, m0 + 4)
                pe.wait_ge(relu_done, 16 * l + 1)
                up(2, m0 + 3).then_inc(used, 1)
                pe.wait_ge(lo_ready, m0 + 5)
                pe.wait_ge(hl_done, 16 * l + 2)
                down(1, m0 + 4).then_inc(used, 1)
                with pe.Fori(1, 7) as it:
                    for i in range(1, 5):
                        m = m0 + i
                        pe.wait_ge(lo_ready, it * 4 + (m + 1))
                        if i % 2:
                            s = (i + 1) // 2
                            pe.wait_ge(relu_done, it * 2 + (16 * l + s - 1))
                            up(s, m).then_inc(used, 1)
                        else:
                            s = i // 2 - 1
                            pe.wait_ge(hl_done, it * 2 + (16 * l + s + 1))
                            down(s, m).then_inc(used, 1)
                pe.wait_ge(lo_ready, m0 + 30)
                pe.wait_ge(relu_done, 16 * l + 14)
                up(15, m0 + 29).then_inc(used, 1)
                pe.wait_ge(lo_ready, m0 + 31)
                pe.wait_ge(hl_done, 16 * l + 15)
                down(14, m0 + 30).then_inc(used, 1)
                pe.wait_ge(lo_ready, m0 + 32)
                pe.wait_ge(hl_done, 16 * l + 16)
                down(15, m0 + 31, last=True)
                sumsq(e, 2)
                if l in (0, 2):
                    mod_sums(l, 0, 10)
                sumsq(e, 3)
                if l in (0, 2):
                    mod_sums(l, 10, 32)

            def scores(ph, i, q, k, r0, masks):
                b = bank[i % 3]
                if i >= 3:
                    pe.wait_ge(s_exp[ph], i - 2)
                rows_ = slice(r0, r0 + 64)
                for t, (c0, c1) in enumerate(((0, 128), (128, 384))):
                    mm(b[:, c0:c1], qk[rows_, q, 128 * t:128 * t + 128], qk[rows_, k, 0:c1 - c0],
                       start=t == 0, stop=False, skip_group_check=True)
                for n, (dst, st, mv) in enumerate(masks):
                    ins = mm(b[:, dst], st, mv, start=False, stop=n == len(masks) - 1, skip_group_check=True)
                ins.then_inc(s_ps[ph], 1)

            causal = [(slice(0, 128), idb[:, :], trib[:, :]), (slice(256, 384), idb[:, :], trib[:, :])]
            chosen = [(slice(0, 384), idb[:, :], sel[:, :])]

            def turn(ph, i, src):
                if i >= 1:
                    pe.wait_ge(s_pt[ph], i)
                for c in range(3):
                    ins = nc.tensor.transpose(bank[3][:, 128 * c:128 * c + 128], src[:, 128 * c:128 * c + 128], ident)
                ins.then_inc(s_tr[ph], 1)

            def values(ph, i, vv, vs, dst):
                pe.wait_ge(s_pt[ph], i + 1)
                p = PT[:, i % 2, :]
                mm(dst[0], p[:, 0:128], vv[:, 0, vs], start=True, stop=True)
                mm(dst[1], p[:, 128:256], vv[:, 0, vs], start=True, stop=False)
                mm(dst[1], p[:, 256:384], vv[:, 1, vs], start=False, stop=True).then_inc(s_pv[ph], 1)

            def turn_out(r, after):
                pe.wait_ge(o_ready, after)
                for j in range(4):
                    for b in (2 * j, 2 * j + 1):
                        for t in range(NT):
                            c = 256 * (b % 2) + 128 * t
                            ins = nc.tensor.transpose(bank[j][:, c:c + 128], o_[:, t, 128 * b:128 * b + 128], ident)
                    ins.then_inc(oT_ready, 1)

            def project(m0, r, e):
                for c in range(4):
                    pe.wait_ge(lo_ready, m0 + c + 1)
                    features(m0 + c, bank[4 + c], (ol_ready, 4 * r, 2) if c == 0 else None).then_inc(acc_ready, 1)
                    slot_free()
                    if c:
                        sumsq(e, c - 1)
                sumsq(e, 3)

            pe.wait_ge(in_x, 16)
            pe.wait_ge(in_con, 16)
            for j in range(4):
                for b in (2 * j, 2 * j + 1):
                    for t in range(NT):
                        c = 256 * (b % 2) + 128 * t
                        ins = nc.tensor.transpose(bank[4 + j][:, c:c + 128], o_[:, t, 128 * b:128 * b + 128], ident)
                ins.then_inc(acc_ready, 1)
            pe.wait_ge(zeroed, 1)
            for j in range(4):
                sumsq(0, j)
            pe.wait_ge(in_rows, 16 * 11)
            nc.tensor.transpose(bank[0][:, 0:NV], rows[0:NV, :], con[0:NV, C_ID:C_ID + NV])
            nc.tensor.transpose(bank[1][:, 0:128], rows2[:, :], ident).then_inc(vec_T, 1)
            pe.wait_ge(in_misc, 64)
            mm(bank[3][0:16, 0:384], relb, hot, start=True, stop=True).then_inc(bias_T, 1)
            order = [0, 1, 3, 4, 5, 6, 7, 8, 9]
            width = {5: 256, 8: 256, 9: 256}

            def swapped(i):
                r = order.index(i)
                w = width.get(i, 512)
                pe.wait_ge(e_t2, r + 1)
                mm(bank[2 + r % 2][:, 0:w], swap, work[:, 2 + r % 2, 0:w], start=True, stop=True).then_inc(e_sw, 1)

            for i in range(10):
                pe.wait_ge(lo_ready, i + 1)
                if i == 2:
                    pe.wait_ge(e_t2, 1)
                    r = i % RING
                    w = [x[:, r, 0:KB * 92].rearrange("p (k n) -> p k n", k=KB) for x in (whi, wlo)]
                    ins = tokens(i, bank[0], 0, 92, w=w)
                elif i in (8, 9):
                    pe.wait_ge(e_t2, order.index(i - 2) + 1)
                    features(i, bank[i % 2], blocks=1)
                    ins = tokens(i, bank[i % 2], 128, 128, o0=256)
                else:
                    if i == 3:
                        pe.wait_ge(e_t2, 2)
                    elif i == 4:
                        pe.wait_ge(gate_in, 1)
                    elif i >= 5:
                        pe.wait_ge(e_t2, order.index(i - 2) + 1)
                    ins = features(i, bank[i % 2], (ul_ready, 0, 1) if i == 0 else None)
                ins.then_inc(used, 1)
                if i - 1 in order:
                    swapped(i - 1)
                if i == 3:
                    pe.wait_ge(e_add, 2)
                    for h in range(4):
                        rr = slice(64 * (h % 2), 64 * (h % 2) + 64)
                        mm(bank[4 + h][:, 0:128], qk[rr, QI + h // 2, 0:128], qk[rr, KI, 0:128], start=True, stop=True)
                        mm(bank[4 + h][:, 128:384], qk[rr, QI + h // 2, 128:256], qk[rr, KI, :], start=True, stop=True)\
                            .then_inc(e_is, 1)
            swapped(9)
            def hidden(kv, half):
                n = PLAIN_AT + 2 * kv + half
                pe.wait_ge(blk_ready, 1)
                pe.wait_ge(loaded[n % RING], loaded_value(n))
                w1 = raw[:, n % RING, :].rearrange("p (k n) -> p k n", k=KB)
                for k in range(KB):
                    ins = mm(bank[7][0:30, 256 * kv:256 * kv + 256], blk[:, kv, KB * half + k, :], w1[:, k, :],
                             start=half == 0 and k == 0, stop=half == 1 and k == KB - 1)
                ins.then_inc(plain_used, 1)

            def turn_hidden():
                pe.wait_ge(h_act, 1)
                for c in range(4):
                    ins = nc.tensor.transpose(bank[6][:, 256 + 30 * c:286 + 30 * c], hact[:, 128 * c:128 * c + 128],
                                              con[0:30, C_ID:C_ID + 30])
                ins.then_inc(hT_ps, 1)

            def compressed_kv():
                pe.wait_ge(in_w2, 48)
                pe.wait_ge(hT_ready, 1)
                for f in range(2):
                    mm(bank[6][:, 0:30], w2[:, f, 0:128], hT[:, f, :], start=f == 0, stop=f == 1)
                for f in range(2):
                    ins = mm(bank[6][0:CW, 64:128], hrep[:, f, :], w2[:, f, 128:192], start=f == 0, stop=f == 1)
                ins.then_inc(kv_ps, 1)

            def compressed_scores():
                pe.wait_ge(kv_ready, 1)
                for t in range(NT):
                    for h in range(8):
                        g = h // 4
                        rr = slice(64 * g, 64 * g + 64)
                        c = 128 + 4 * NBLK * t + NBLK * (h % 4)
                        ins = mm(bank[6 + g][:, c:c + NBLK],
                                 qk[rr, QB + h % 4, 128 * t:128 * t + 128], kcm[rr, NBLK * g:NBLK * g + NBLK],
                                 start=True, stop=True)
                ins.then_inc(sc_ps, 1)

            pe.wait_ge(e_add, 9)
            pe.wait_ge(e_sel, 1)
            for i in range(24 + 3):
                if i < 24:
                    q, r0, k, vv, vs, ob = even_map(i)
                    scores("e", i, q, k, r0, causal + chosen if i < 8 else causal)
                if i < 4:
                    hidden(i // 2, i % 2)
                if i == 5:
                    turn_hidden()
                if i == 6:
                    compressed_kv()
                if i == 7:
                    compressed_scores()
                if i >= 3:
                    j = i - 3
                    q, r0, k, vv, vs, ob = even_map(j)
                    if j == 8:
                        pe.wait_ge(sc_sub, 1)
                    if j == 16:
                        pe.wait_ge(o_free, 1)
                    hs = slice(64 * (j % 8), 64 * (j % 8) + 64)
                    values("e", j, vv, vs, [bank[ob[0]][:, hs], bank[ob[1]][:, hs]])
                if 2 <= i < 26:
                    pe.wait_ge(s_exp["e"], i - 1)
                    turn("e", i - 2, P[:, (i - 2) % 4, :])
                if i == 11:
                    for t in range(NT):
                        pe.wait_ge(pc_ready, t + 1)
                        pe.wait_ge(s_pt["e"], 10)
                        if t:
                            pe.wait_ge(pcT_ready, t)
                        nc.tensor.transpose(bank[3][0:CW, 384:512], pc[:, t, :], ident).then_inc(pc_ps, 1)
                    pe.wait_ge(pcT_ready, NT)
                if i == 23:
                    pe.wait_ge(o_free, 2)
                    for t in range(NT):
                        ins = mm(bank[6 + t][:, :], pcT[0:CW, t, :], vbd[0:CW, :, :], start=True, stop=True)
                    ins.then_inc(oc_ps, 1)
            turn_out(0, NT)
            project(MLP0 - 4, 0, 1)
            mlp(0)

            def dswap(i):
                pe.wait_ge(d_t2, i + 1)
                mm(bank[2 + i % 2][:, :], swap, work[:, 2 + i % 2, :], start=True, stop=True).then_inc(d_sw, 1)

            for i in range(12):
                pe.wait_ge(lo_ready, DIFF + i + 1)
                if 2 <= i < 10:
                    pe.wait_ge(d_t2, i - 1)
                elif i >= 10:
                    pe.wait_ge(d_v, i - 9)
                if i < 8:
                    features(DIFF + i, bank[i % 2], (ul_ready, ul_no(2), 1) if i == 0 else None).then_inc(used, 1)
                else:
                    tokens(DIFF + i, bank[i % 2], 0, 256).then_inc(used, 1)
                if i == 1:
                    pe.wait_ge(mod_ready, 1)
                if 1 <= i <= 8:
                    dswap(i - 1)
            pe.wait_ge(d_add, 8)
            pe.wait_ge(d_v, 4)
            for i in range(8 + 2):
                if i < 8:
                    for c in range(2):
                        scores("d", 2 * i + c, i, 8 + i, 64 * c, causal)
                if i >= 2:
                    j = i - 2
                    hs = slice(128 * (j % 4), 128 * (j % 4) + 128)
                    values("d", j, v_, slice(128 * j, 128 * j + 128), [bank[4 + j // 4][:, hs], bank[6 + j // 4][:, hs]])
                if 1 <= i < 9:
                    pe.wait_ge(s_cmb, i)
                    turn("d", i - 1, P[:, 2 * (i - 1) % 4, :])
            turn_out(1, 2 * NT)
            project(MLP1 - 4, 1, 3)
            mlp(1)
            for j in range(4):
                sumsq(5, j)
            mod_sums(1, 0, 32)

            pe.wait_ge(lo_ready, POOL + 1)
            wp = [x[:, POOL % RING, :].rearrange("p (g k n) -> p g k n", g=4, k=2) for x in (whi, wlo)]
            for g in range(4):
                pe.wait_ge(p_h, g + 1)
                for b in range(2):
                    for k in range(2):
                        c = slice(128 * b, 128 * b + 128)
                        ins = three(bank[4 + g][:, 256 * b:256 * b + 256], True, wp[0][:, g, k, c], wp[1][:, g, k, c],
                                    uh[:, 2 * g + k, :], ul[:, 2 * g + k, :], b == 0 and k == 0, k == 1)
                ins.then_inc(acc_ready, 1)
            pe.wait_ge(mod_ready, 2)
            slot_free()
            for j in range(4):
                sumsq(6, j)
            mlp(2)

            for i in range(12):
                pe.wait_ge(lo_ready, MOBA + i + 1)
                if i >= 2:
                    pe.wait_ge(b_copied, i - 1)
                if i < 8:
                    features(MOBA + i, bank[i % 2], (ul_ready, ul_no(7), 1) if i == 0 else None).then_inc(used, 1)
                else:
                    tokens(MOBA + i, bank[i % 2], 0, 256).then_inc(used, 1)
            pe.wait_ge(b_copied, 12)
            pe.wait_ge(mod_ready, 3)
            for i in range(16 + 3):
                if i < 16:
                    pe.wait_ge(h_in[i % 8], 16 * (i // 8 + 1))
                    scores("b", i, i // 2, 8 + i // 2, 64 * (i % 2),
                           [(slice(0, 128), flip, hank[:, i % 8, 128:256]), (slice(128, 384), flip, hank[:, i % 8, :])])
                if i >= 3:
                    j = i - 3
                    hs = slice(64 * (j % 8), 64 * (j % 8) + 64)
                    values("b", j, v_, slice(64 * j, 64 * j + 64), [bank[4 + j // 8][:, hs], bank[6 + j // 8][:, hs]])
                if 2 <= i < 18:
                    pe.wait_ge(s_exp["b"], i - 1)
                    turn("b", i - 2, P[:, (i - 2) % 4, :])
            turn_out(2, 3 * NT)
            project(MLP3 - 4, 2, 8)
            mlp(3)
            pe.wait_ge(u_ready, u_no(9) + 8)
            for t in range(NT):
                for c in range(2):
                    for b in range(4):
                        ins = nc.tensor.transpose(bank[4 + 2 * t + c][:, 128 * b:128 * b + 128],
                                                  u[:, 4 * c + b, 128 * t:128 * t + 128], ident)
                    ins.then_inc(fin_T, 1)


def constants():
    con = np.zeros((128, C_END), np.float32)
    p = np.arange(128)
    con[p, C_ID + p] = 1
    con[p, C_SW + (p ^ 32)] = 1
    con[p, C_FLIP + 127 - p] = 1
    con[:, C_TRI:C_TRI + 128] = np.where(p[None, :] > p[:, None], np.float32(MARK), np.float32(0))
    inv = (1.0 / (np.float32(10000.0) ** (np.arange(0, HD, 2, dtype=np.float32) / np.float32(HD)))).astype(np.float32)
    ang = np.arange(T, dtype=np.float32)[None, :] * inv[p % 32][:, None]
    cos, sin = np.cos(ang).astype(np.float32), np.sin(ang).astype(np.float32)
    sin = np.where((p % 64 < 32)[:, None], sin, -sin)
    con[:, C_COS:C_COS + T], con[:, C_SIN:C_SIN + T] = cos, sin
    con[:, C_COSQ:C_COSQ + T], con[:, C_SINQ:C_SINQ + T] = cos * np.float32(0.125), sin * np.float32(0.125)
    for b in range(KB):
        w = 2 << (b // 2)
        t = np.arange(16)
        con[:, C_CORR + 16 * b:C_CORR + 16 * b + 16] = (w / np.minimum(t + 1, w)).astype(np.float32)
    for h in range(8):
        con[NBLK * h:NBLK * h + NBLK, C_HB + h] = 1
    for t in range(NT):
        end = 16 * np.arange(NBLK) + 31
        con[:, C_CMP + NBLK * t:C_CMP + NBLK * t + NBLK] = end[None, :] <= (128 * t + p)[:, None]
    dist = 255 - np.arange(384)
    d = np.maximum(dist, 0)
    nf = np.maximum(d, 1).astype(np.float32)
    large = 16 + (np.log(nf / np.float32(16)) / np.float32(math.log(64)) * np.float32(16)).astype(np.int32)
    bucket = np.where(d < 16, d, np.minimum(large, 31))
    hot = np.zeros((32, 384), np.float32)
    hot[bucket, np.arange(384)] = dist >= 0
    gmask = np.broadcast_to(np.where(dist >= 0, np.float32(0), np.float32(NEG)), (16, 384))
    return con, hot, np.ascontiguousarray(gmask)


def kernel(**inputs):
    import numpy as _np
    import concourse.bacc as _bacc
    from concourse import mybir as _mybir
    from concourse.bass_utils import run_bass_kernel_spmd as _run

    f32 = _mybir.dt.float32
    g = {k: _np.ascontiguousarray(_np.asarray(v)) for k, v in inputs.items()}
    con, hot, gmask = constants()
    arrays = {
        "x": g["x"].reshape(T, D), "con": con, "hot": hot, "gmask": gmask,
        "even_in": g["even_w_in"][0], "cmp_w1": g["even_cmp_w1"][0], "cmp_w2": g["even_cmp_w2"][0],
        "cmp_pe": g["even_cmp_pe"].reshape(-1), "even_out": g["even_w_out"][0],
        "odd_in": g["odd_w_in"][0], "odd_out": g["odd_w_out"][0], "lam": g["odd_lambda"][0], "sub_g": g["odd_subln_g"].reshape(-1),
        "mix_g": g["mix_norm_g"].reshape(-1), "mlp_g": g["mlp_norm_g"].reshape(-1), "fin_g": g["final_norm_g"],
        "mix_g2": g["norm_mix_2"].reshape(-1), "mlp_g2": g["norm_mlp_2"].reshape(-1), "fin_g2": g["norm_final_2"],
        "pool_s": g["pool_scale_2"].reshape(-1), "c": g["c_2"].reshape(-1), "b_mod": g["b_mod_2"].reshape(-1),
        "rel_bias": g["rel_bias_2"], "w_mod": g["w_mod_2"], "w_pool": g["w_pool_2"][0], "w_qkv": g["w_qkv_2"][0],
        "w_o": g["w_o_2"][0], "up_a": g["mlp_w_up"], "down_a": g["mlp_w_down"], "up_b": g["w_up_2"], "down_b": g["w_down_2"],
    }
    nc = _bacc.Bacc("TRN2", target_bir_lowering=False, num_devices=1)
    ap = {k: nc.dram_tensor(f"in_{k}", v.shape, f32, kind="ExternalInput").ap() for k, v in arrays.items()}
    ap["up"] = [ap["up_a"][0], ap["up_a"][1], ap["up_b"][0], ap["up_b"][1]]
    ap["down"] = [ap["down_a"][0], ap["down_a"][1], ap["down_b"][0], ap["down_b"][1]]
    ap["out"] = nc.dram_tensor("out_y", (T, D), f32, kind="ExternalOutput").ap()
    build(nc, ap)
    r = _run(nc, [{f"in_{k}": v for k, v in arrays.items()}], core_ids=[0])
    return r.results[0]["out_y"].reshape(1, T, D)
```
